# Optimizing a Trainium2 kernel written in Bass

```python
import jax, jax.numpy as jnp
from jax import lax
import numpy as np

D_MODEL = 1024
BATCH = 1
SEQ = 1024
DEPTH = 1

N_MIXERS = 3
NORM_EPS = 1e-6
POOL_WINDOWS = (2, 4, 8, 16)
POOL_GROUPS = len(POOL_WINDOWS)
POOL_CH = D_MODEL // POOL_GROUPS
SCONV_WIDTH = 3
SSM_EXPAND = 2
SSM_D_INNER = SSM_EXPAND * D_MODEL
SSM_HEAD_DIM = 64
SSM_HEADS = SSM_D_INNER // SSM_HEAD_DIM
SSM_GROUPS = 4
SSM_STATE = 128
SSM_CONV_WIDTH = 4
SSM_CHUNK = 128
SSM_CONV_DIM = SSM_D_INNER + 2 * SSM_GROUPS * SSM_STATE
SSM_IN_DIM = SSM_D_INNER + SSM_CONV_DIM + SSM_HEADS
MOE_GROUPS = 4
MOE_EXPERTS_PER_GROUP = 8
MOE_EXPERTS = MOE_GROUPS * MOE_EXPERTS_PER_GROUP
MOE_TOP_K = 2
MOE_D_FF = 512
MOE_BLOCK = 128
N_POOL_LAYERS = len(range(0, DEPTH, N_MIXERS))
N_SCONV_LAYERS = len(range(1, DEPTH, N_MIXERS))
N_SSM_LAYERS = len(range(2, DEPTH, N_MIXERS))

kernel_name = "hybrid_pool_conv_ssd_hmoe"

def rms_norm(x, w):
    xf = x.astype(jnp.float32)
    y = xf * lax.rsqrt(jnp.mean(xf * xf, axis=-1, keepdims=True) + NORM_EPS)
    return (y * w.astype(jnp.float32)).astype(x.dtype)

def causal_depthwise_conv(u, w):
    k, c = w.shape
    return lax.conv_general_dilated(
        u, w[:, None, :].astype(u.dtype), window_strides=(1,),
        padding=[(k - 1, 0)], dimension_numbers=("NWC", "WIO", "NWC"),
        feature_group_count=c)

def pool_mixer(h, w_grp, scale):
    bsz, s, d = h.shape
    hg = h.astype(jnp.float32).reshape(bsz, s, POOL_GROUPS, POOL_CH)
    csum = jnp.cumsum(hg, axis=1)
    outs = []
    for g, win in enumerate(POOL_WINDOWS):
        c = csum[:, :, g]
        lagged = jnp.pad(c, ((0, 0), (win, 0), (0, 0)))[:, :s]
        count = jnp.minimum(jnp.arange(1, s + 1), win).astype(jnp.float32)[None, :, None]
        outs.append((c - lagged) / count - hg[:, :, g])
    pooled = jnp.stack(outs, axis=2).astype(h.dtype)
    y = jnp.einsum("bsgc,gcd->bsgd", pooled, w_grp).reshape(bsz, s, d)
    return y * scale

def short_conv_mixer(h, w_in, taps, w_out):
    b_gate, c_gate, v = jnp.split(h @ w_in, 3, axis=-1)
    u = causal_depthwise_conv(c_gate * v, taps)
    return (b_gate * u) @ w_out

def ssd_chunked(x, a, b, c):
    bsz, s, nh, p = x.shape
    g, n = b.shape[2], b.shape[3]
    r = nh // g
    q = SSM_CHUNK
    nc = s // q
    x = x.reshape(bsz, nc, q, g, r, p)
    a = a.reshape(bsz, nc, q, g, r).transpose(0, 1, 3, 4, 2)
    b = b.reshape(bsz, nc, q, g, n)
    c = c.reshape(bsz, nc, q, g, n)
    a_cs = jnp.cumsum(a, axis=-1)
    causal = jnp.tril(jnp.ones((q, q), dtype=bool))
    seg = a_cs[..., :, None] - a_cs[..., None, :]
    decay = jnp.exp(jnp.where(causal, seg, -jnp.inf))
    cb = jnp.einsum("bclgn,bcsgn->bcgls", c, b)
    y_diag = jnp.einsum("bcgrls,bcsgrp->bclgrp", cb[:, :, :, None] * decay, x)
    decay_states = jnp.exp(a_cs[..., -1:] - a_cs).transpose(0, 1, 4, 2, 3)[..., None]
    states = jnp.einsum("bclgn,bclgrp->bcgrpn", b, x * decay_states)
    chunk_decay = jnp.exp(a_cs[..., -1])

    def step(carry, inp):
        st, dec = inp
        return carry * dec[..., None, None] + st, carry

    init = jnp.zeros((bsz, g, r, p, n), dtype=x.dtype)
    _, prev = lax.scan(step, init, (states.transpose(1, 0, 2, 3, 4, 5),
                                    chunk_decay.transpose(1, 0, 2, 3)))
    prev = prev.transpose(1, 0, 2, 3, 4, 5)
    out_decay = jnp.exp(a_cs).transpose(0, 1, 4, 2, 3)[..., None]
    y_off = jnp.einsum("bclgn,bcgrpn->bclgrp", c, prev) * out_decay
    return (y_diag + y_off).reshape(bsz, s, nh, p)

def mamba2_mixer(h, w_in, conv_w, conv_b, dt_bias, a_log, d_skip, norm_w, w_out):
    bsz, s, _ = h.shape
    f32 = jnp.float32
    z, xbc, dt = jnp.split(h @ w_in, [SSM_D_INNER, SSM_D_INNER + SSM_CONV_DIM], axis=-1)
    xbc = jax.nn.silu(causal_depthwise_conv(xbc, conv_w) + conv_b)
    xs, bm, cm = jnp.split(xbc, [SSM_D_INNER, SSM_D_INNER + SSM_GROUPS * SSM_STATE], axis=-1)
    dt = jax.nn.softplus(dt.astype(f32) + dt_bias.astype(f32))
    a = -jnp.exp(a_log.astype(f32))
    xh = xs.astype(f32).reshape(bsz, s, SSM_HEADS, SSM_HEAD_DIM)
    y = ssd_chunked(xh * dt[..., None], dt * a,
                    bm.astype(f32).reshape(bsz, s, SSM_GROUPS, SSM_STATE),
                    cm.astype(f32).reshape(bsz, s, SSM_GROUPS, SSM_STATE))
    y = y + xh * d_skip.astype(f32)[:, None]
    y = y.reshape(bsz, s, SSM_D_INNER) * jax.nn.silu(z.astype(f32))
    yg = y.reshape(bsz, s, SSM_GROUPS, SSM_D_INNER // SSM_GROUPS)
    yg = yg * lax.rsqrt(jnp.mean(yg * yg, axis=-1, keepdims=True) + NORM_EPS)
    y = (yg.reshape(bsz, s, SSM_D_INNER) * norm_w.astype(f32)).astype(h.dtype)
    return y @ w_out

def grouped_expert_ffn(xt, expert, gate, w_gu, w_dn):
    t, d = xt.shape
    k = expert.shape[1]
    n_exp = w_gu.shape[0]
    n_assign = t * k
    flat_e = expert.reshape(-1)
    flat_tok = jnp.arange(n_assign, dtype=jnp.int32) // k
    flat_w = gate.reshape(-1)
    order = jnp.argsort(flat_e)
    sorted_e = flat_e[order]
    counts = jnp.bincount(flat_e, length=n_exp)
    padded = (counts + MOE_BLOCK - 1) // MOE_BLOCK * MOE_BLOCK
    pad_end = jnp.cumsum(padded)
    pad_start = pad_end - padded
    start = jnp.cumsum(counts) - counts
    dest = pad_start[sorted_e] + (jnp.arange(n_assign, dtype=jnp.int32) - start[sorted_e])
    n_rows = (n_assign + MOE_BLOCK - 1) // MOE_BLOCK * MOE_BLOCK + n_exp * MOE_BLOCK
    n_blocks = n_rows // MOE_BLOCK
    buf_tok = jnp.full((n_rows,), t, dtype=jnp.int32).at[dest].set(flat_tok[order])
    buf_w = jnp.zeros((n_rows,), dtype=xt.dtype).at[dest].set(flat_w[order])
    block_e = jnp.minimum(
        jnp.searchsorted(pad_end, jnp.arange(n_blocks) * MOE_BLOCK, side="right"), n_exp - 1)
    x_pad = jnp.concatenate([xt, jnp.zeros((1, d), dtype=xt.dtype)], axis=0)
    xb = x_pad[buf_tok].reshape(n_blocks, MOE_BLOCK, d)

    def expert_block(args):
        xblk, e = args
        g_part, up = jnp.split(xblk @ w_gu[e], 2, axis=-1)
        return (jax.nn.silu(g_part) * up) @ w_dn[e]

    yb = lax.map(expert_block, (xb, block_e)).reshape(n_rows, d)
    out = jnp.zeros((t + 1, d), dtype=xt.dtype).at[buf_tok].add(yb * buf_w[:, None])
    return out[:t]

def hier_moe(h, w_rg, b_rg, w_re, b_re, w_gu, w_dn):
    bsz, s, d = h.shape
    t = bsz * s
    xt = h.reshape(t, d)
    g_logits = (xt @ w_rg).astype(jnp.float32) + b_rg.astype(jnp.float32)
    g_prob = jax.nn.softmax(g_logits, axis=-1)
    g_sel = jnp.argmax(g_logits, axis=-1)
    p_group = jnp.take_along_axis(g_prob, g_sel[:, None], axis=1)
    e_logits = ((xt @ w_re).astype(jnp.float32) + b_re.astype(jnp.float32)).reshape(
        t, MOE_GROUPS, MOE_EXPERTS_PER_GROUP)
    e_logits = jnp.take_along_axis(e_logits, g_sel[:, None, None], axis=1)[:, 0]
    e_prob = jax.nn.softmax(e_logits, axis=-1)
    top_p, top_i = lax.top_k(e_prob, MOE_TOP_K)
    gate = (p_group * top_p / jnp.sum(top_p, axis=-1, keepdims=True)).astype(h.dtype)
    expert = (g_sel[:, None] * MOE_EXPERTS_PER_GROUP + top_i).astype(jnp.int32)
    return grouped_expert_ffn(xt, expert, gate, w_gu, w_dn).reshape(bsz, s, d)

def setup_inputs(seed: int = 0) -> dict:
    key = jax.random.key(seed)
    ks = jax.random.split(key, 24)
    f32 = jnp.float32
    d = D_MODEL

    def nrm(k, shape, fan_in):
        return jax.random.normal(k, shape, f32) * (fan_in ** -0.5)

    def gain(k, shape):
        return 1.0 + 0.05 * jax.random.normal(k, shape, f32)

    dt0 = jnp.exp(jax.random.uniform(ks[13], (N_SSM_LAYERS, SSM_HEADS), f32)
                  * (np.log(0.1) - np.log(0.001)) + np.log(0.001))
    dt_bias = dt0 + jnp.log(-jnp.expm1(-dt0))
    a_log = jnp.log(jax.random.uniform(ks[14], (N_SSM_LAYERS, SSM_HEADS), f32, 1.0, 16.0))
    return {
        "x": jax.random.normal(ks[0], (BATCH, SEQ, d), f32),
        "norm_mix": gain(ks[1], (DEPTH, d)),
        "norm_ffn": gain(ks[2], (DEPTH, d)),
        "norm_final": gain(ks[3], (d,)),
        "pool_w": nrm(ks[4], (N_POOL_LAYERS, POOL_GROUPS, POOL_CH, POOL_CH), POOL_CH),
        "pool_scale": gain(ks[5], (N_POOL_LAYERS, d)),
        "sconv_in_w": nrm(ks[6], (N_SCONV_LAYERS, d, 3 * d), d),
        "sconv_taps": nrm(ks[7], (N_SCONV_LAYERS, SCONV_WIDTH, d), SCONV_WIDTH),
        "sconv_out_w": nrm(ks[8], (N_SCONV_LAYERS, d, d), d),
        "ssm_in_w": nrm(ks[9], (N_SSM_LAYERS, d, SSM_IN_DIM), d),
        "ssm_conv_w": nrm(ks[10], (N_SSM_LAYERS, SSM_CONV_WIDTH, SSM_CONV_DIM), SSM_CONV_WIDTH),
        "ssm_conv_b": 0.01 * jax.random.normal(ks[11], (N_SSM_LAYERS, SSM_CONV_DIM), f32),
        "ssm_dt_bias": dt_bias,
        "ssm_a_log": a_log,
        "ssm_d": gain(ks[12], (N_SSM_LAYERS, SSM_HEADS)),
        "ssm_norm_w": gain(ks[15], (N_SSM_LAYERS, SSM_D_INNER)),
        "ssm_out_w": nrm(ks[16], (N_SSM_LAYERS, SSM_D_INNER, d), SSM_D_INNER),
        "router_group_w": nrm(ks[17], (DEPTH, d, MOE_GROUPS), d),
        "router_group_b": 0.01 * jax.random.normal(ks[18], (DEPTH, MOE_GROUPS), f32),
        "router_expert_w": nrm(ks[19], (DEPTH, d, MOE_EXPERTS), d),
        "router_expert_b": 0.01 * jax.random.normal(ks[20], (DEPTH, MOE_EXPERTS), f32),
        "expert_w_gu": nrm(ks[21], (DEPTH, MOE_EXPERTS, d, 2 * MOE_D_FF), d),
        "expert_w_down": nrm(ks[22], (DEPTH, MOE_EXPERTS, MOE_D_FF, d), MOE_D_FF),
    }

def reference(x, norm_mix, norm_ffn, norm_final, pool_w, pool_scale,
              sconv_in_w, sconv_taps, sconv_out_w,
              ssm_in_w, ssm_conv_w, ssm_conv_b, ssm_dt_bias, ssm_a_log, ssm_d,
              ssm_norm_w, ssm_out_w,
              router_group_w, router_group_b, router_expert_w, router_expert_b,
              expert_w_gu, expert_w_down):
    for i in range(DEPTH):
        kind, j = i % N_MIXERS, i // N_MIXERS
        h = rms_norm(x, norm_mix[i])
        if kind == 0:
            mix = pool_mixer(h, pool_w[j], pool_scale[j])
        elif kind == 1:
            mix = short_conv_mixer(h, sconv_in_w[j], sconv_taps[j], sconv_out_w[j])
        else:
            mix = mamba2_mixer(h, ssm_in_w[j], ssm_conv_w[j], ssm_conv_b[j], ssm_dt_bias[j],
                               ssm_a_log[j], ssm_d[j], ssm_norm_w[j], ssm_out_w[j])
        x = x + mix
        x = x + hier_moe(rms_norm(x, norm_ffn[i]), router_group_w[i], router_group_b[i],
                         router_expert_w[i], router_expert_b[i],
                         expert_w_gu[i], expert_w_down[i])
    return rms_norm(x, norm_final)


_drawn_inputs = setup_inputs


def setup_inputs(seed=0):
    import zlib

    import numpy as np

    out = dict(_drawn_inputs(seed))
    spreads = {}
    factors = {'router_group_b': 3.305, 'router_expert_b': 4.576}
    for name, (base, spread) in spreads.items():
        noise = np.random.default_rng([zlib.crc32(name.encode()), seed]).standard_normal(out[name].shape)
        drawn = base * np.exp(spread * noise) if base else spread * noise
        out[name] = __import__('jax').numpy.asarray(drawn.astype(out[name].dtype))
    for name, factor in factors.items():
        out[name] = (out[name] * factor).astype(out[name].dtype)
    return out
```

```python
from contextlib import ExitStack

import numpy as np

import concourse.bass as bass
from concourse import mybir


def hybrid_pool_moe(nc, x, norm_mix, norm_ffn, norm_final, pool_w, pool_scale,
                    w_rg, b_rg, w_re, b_re, w_gu, w_down, out):
    f32, f32r, bf16 = mybir.dt.float32, mybir.dt.float32r, mybir.dt.bfloat16
    i32, u32 = mybir.dt.int32, mybir.dt.uint32
    ALU, ACT, AX = mybir.AluOpType, mybir.ActivationFunctionType, mybir.AxisListType.X

    P = 128
    TOKENS, D = x.shape[1], x.shape[2]
    TILES = TOKENS // P
    EPS = 1e-6
    WINDOWS = (2, 4, 8, 16)
    HALO = WINDOWS[-1]
    NG = w_rg.shape[2]
    E = w_re.shape[2]
    NJ = E // NG
    NL = NG + E
    K = 2
    F = w_down.shape[2]
    KD, KF = D // P, F // P
    N = 512
    OVERFLOW = K * TOKENS // P - 1
    BLOCKS = E + OVERFLOW + 1
    FAR = 100000.0
    PAIR = 2 * D
    PER_STEP = (KD + KF) // 2
    GU_PAIRS = KD // 2
    RAW, SPLIT = 2 * PER_STEP, 3

    gu_rows = w_gu[0].rearrange("e (p k) f -> e p (k f)", k=KD)
    dn_rows = w_down[0].rearrange("e (p k) d -> e p (k d)", k=KF)
    x_rows = x[0]
    out_rows = out[0]

    normed = nc.dram_tensor("normed", [TOKENS, D], f32).ap()
    expert_out = nc.dram_tensor("expert_out", [K * TOKENS, D], f32).ap()

    ctx = ExitStack()
    with ctx:
        def sem(name):
            return ctx.enter_context(nc.semaphore(name))

        KB = 1024
        ARENA = 204 * KB
        base = (nc.sbuf_base + 31) // 32 * 32
        ctx.enter_context(nc.sbuf_tensor("arena", [P, ARENA // 4], f32))

        def at(name, shape, dt, offset):
            return nc.alloc_sbuf_tensor_at(name, shape, dt, offset=base + offset)

        def small(name, shape, dt):
            return ctx.enter_context(nc.sbuf_tensor(name, shape, dt))

        raw = at("raw", [P, RAW, PAIR], f32, 0)
        HI, LO, RES, WORK = 96 * KB, 120 * KB, 144 * KB, 176 * KB
        w_hi = at("w_hi", [P, SPLIT, PAIR], f32r, HI)
        w_lo = at("w_lo", [P, SPLIT, PAIR], f32r, LO)
        res = at("res", [P, TILES, D], f32, RES)
        xg = at("xg", [P, 2, D], f32, WORK)
        x_hi = at("x_hi", [P, KD, P], f32r, WORK + 8 * KB)
        x_lo = at("x_lo", [P, KD, P], f32r, WORK + 12 * KB)
        silu = at("silu", [P, F], f32, WORK + 16 * KB)
        hid = at("hid", [P, KF, P], f32, WORK + 18 * KB)
        h_hi = at("h_hi", [P, KF, P], f32r, WORK + 20 * KB)
        h_lo = at("h_lo", [P, KF, P], f32r, WORK + 22 * KB)
        ysb = at("ysb", [P, D], f32, WORK + 24 * KB)
        xs_hi = at("xs_hi", [P, 2, D], f32r, HI)
        xs_lo = at("xs_lo", [P, 2, D], f32r, HI + 8 * KB)
        pt_hi = at("pt_hi", [P, KD, P], f32r, HI + 16 * KB)
        pt_lo = at("pt_lo", [P, KD, P], f32r, HI + 20 * KB)
        pw_hi = at("pw_hi", [P, KD, 2 * P], f32r, LO)
        pw_lo = at("pw_lo", [P, KD, 2 * P], f32r, LO + 8 * KB)
        band = at("band", [P, NG, P], f32r, LO + 16 * KB)
        band0 = at("band0", [P, NG, P], f32r, LO + 18 * KB)
        halo = at("halo", [P, NG, HALO], f32r, LO + 20 * KB)
        nx = at("nx", [P, 2, KD, P], f32, WORK)
        nxT = at("nxT", [P, 2, KD, P], f32, WORK + 8 * KB)
        nf_all = at("nf_all", [P, D], f32, WORK + 24 * KB)
        junk = at("junk", [P, D], bf16, WORK + 22 * KB)
        RW = (RAW - 3) * 4 * PAIR
        pw_in = at("pw_in", [P, KD, 2 * P], f32, RW)
        pw = at("pw", [P, KD, 2 * P], f32, RW + 8 * KB)
        sc_all = at("sc_all", [P, D], f32, RW + 16 * KB)
        band_w = at("band_w", [P, NG, P], f32, RW + 20 * KB)
        halo_w = at("halo_w", [P, NG, HALO], f32, RW + 22 * KB)
        nm_rows = at("nm_rows", [KD, P], f32, RW + 23 * KB)
        wr_g = at("wr_g", [P, KD * NG], f32, WORK + 16 * KB)
        wr_e = at("wr_e", [P, KD * E], f32, WORK + 16 * KB + 128)
        wr = at("wr", [P, KD, NL], f32, WORK + 18 * KB)
        tri_f = at("tri_f", [P, P], f32, WORK + 20 * KB)
        tri = at("tri", [P, P], bf16, WORK + 20 * KB + 512)
        ones = at("ones", [P, P], bf16, WORK + 20 * KB + 768)
        cursor = [WORK + 21 * KB]

        def tmp(name, shape, dt=f32):
            size = int(np.prod(shape)) * (2 if dt == bf16 else 4)
            here = cursor[0]
            cursor[0] += (size + 31) // 32 * 32
            assert cursor[0] <= ARENA, name
            return at(name, [P] + list(shape), dt, here)

        iota_b = tmp("iota_b", [BLOCKS])
        iota_p = tmp("iota_p", [P])
        val = tmp("val", [K, TILES])
        steps7 = tmp("steps7", [OVERFLOW // 2])
        chosen = tmp("chosen", [TILES + 1, E], bf16)
        t8 = [tmp(f"t8_{n}", [TILES]) for n in range(8)]
        t32 = [tmp(f"t32_{n}", [TILES, NG]) for n in range(2)]
        t64 = [tmp(f"t64_{n}", [TILES, NJ]) for n in range(6)]
        e32 = [tmp(f"e32_{n}", [E]) for n in range(5)]
        blk = tmp("blk", [K, TILES])
        row = tmp("row", [K, TILES])
        gexp = tmp("gexp", [TILES, NG])
        slot = tmp("slot", [BLOCKS])
        slot2 = tmp("slot2", [BLOCKS])
        first_g = tmp("first_g", [TILES, NG])
        cursor[0] = WORK + 8 * KB
        is_row = tmp("is_row", [K * TILES, P], f32r)
        cursor[0] = HI
        pick = tmp("pick", [K, TILES, E])
        prod = tmp("prod", [K, TILES, E])
        rank = tmp("rank", [TILES + 1, E])
        rank_i = tmp("rank_i", [TILES, E], i32)
        quot_i = tmp("quot_i", [TILES, E], i32)
        rem_i = tmp("rem_i", [TILES, E], i32)
        quot = tmp("quot", [TILES, E])
        rem = tmp("rem", [TILES, E])
        blk_of = tmp("blk_of", [TILES, E])
        over = tmp("over", [E, OVERFLOW // 2])
        late = tmp("late", [OVERFLOW + 1, E])
        byg = tmp("byg", [TILES, NG, NJ])
        is_blk = tmp("is_blk", [K * TILES, BLOCKS])
        is_val = tmp("is_val", [K * TILES, BLOCKS], f32r)
        assert cursor[0] <= HI + 24 * KB

        ident = small("ident", [P, P], f32)
        logit = small("logit", [P, TILES, NL], f32)
        bias = small("bias", [P, NL], f32)
        ss = small("ss", [P, TILES], f32)
        rs = small("rs", [P, TILES], f32)
        ss2 = small("ss2", [P, TILES], f32)
        rs2 = small("rs2", [P, TILES], f32)
        count0 = small("count0", [P, NG], f32)
        ncount0 = small("ncount0", [P, NG], f32)
        fix0 = small("fix0", [P, NG], f32)
        eps = small("eps", [P, 1], f32)
        nm = small("nm", [P, KD], f32)
        gate = small("gate", [P, K, TILES], f32)
        src_all = small("src_all", [P, BLOCKS], i32)
        dst_all = small("dst_all", [P, BLOCKS], i32)
        src_now = small("src_now", [P, 2], i32)
        dst_now = small("dst_now", [P, 1], i32)
        over_e = small("over_e", [P, OVERFLOW + 1], i32)
        n_over = small("n_over", [P, 1], i32)

        psum = ctx.enter_context(nc.psum_tensor("psum", [P, 8, N], f32))
        bank = lambda b, n=1: psum[:, b:b + n, :].rearrange("p b n -> p (b n)")
        PT, PY, NXT, LG, MISC = bank(0, 2), bank(2, 2), bank(4, 2), bank(6), bank(7)
        GU, Y, XT, HT = bank(0, 2), bank(2, 2), bank(4, 2), bank(6)

        x_in = [sem(f"x_in{i}") for i in range(TILES)]
        mix_w_in = sem("mix_w_in")
        router_w_in = sem("router_w_in")
        nf_in = sem("nf_in")
        consts = sem("consts")
        dve_step = sem("dve_step")
        act_step = sem("act_step")
        nm_turned = sem("nm_turned")
        pw_made = sem("pw_made")
        pw_hi_done = sem("pw_hi_done")
        pw_split = sem("pw_split")
        squares = sem("squares")
        scales = sem("scales")
        xs_hi_done = sem("xs_hi_done")
        xs_split = sem("xs_split")
        pooled = sem("pooled")
        pt_hi_done = sem("pt_hi_done")
        pt_split = sem("pt_split")
        mixed = sem("mixed")
        res_made = sem("res_made")
        squares2 = sem("squares2")
        nx_made = sem("nx_made")
        nx_turned = sem("nx_turned")
        nxT_copied = sem("nxT_copied")
        nx_stored = [sem(f"nx_stored{i}") for i in range(2)]
        logits_done = sem("logits_done")
        g_shift = sem("g_shift")
        g_exp = sem("g_exp")
        e_shift = sem("e_shift")
        e_exp = sem("e_exp")
        chosen_made = sem("chosen_made")
        ranked = sem("ranked")
        rows_made = sem("rows_made")
        slotted = sem("slotted")
        tables_made = sem("tables_made")
        raw_in = [sem(f"raw_in{i}") for i in range(RAW)]
        hi_done = sem("hi_done")
        lo_done = sem("lo_done")
        pair_used = sem("pair_used")
        idx_now = sem("idx_now")
        gathered = [sem(f"gathered{i}") for i in range(2)]
        xg_clear = sem("xg_clear")
        x_turned = sem("x_turned")
        x_hi_done = sem("x_hi_done")
        x_split = sem("x_split")
        silu_done = sem("silu_done")
        hid_made = sem("hid_made")
        hid_turned = sem("hid_turned")
        h_hi_done = sem("h_hi_done")
        h_split = sem("h_split")
        y_copied = sem("y_copied")
        y_stored = sem("y_stored")
        y_in = [sem(f"y_in{i}") for i in range(TILES)]
        nfin_in = sem("nfin_in")
        total_made = sem("total_made")
        squares3 = sem("squares3")
        scales3 = sem("scales3")
        scaled3 = sem("scaled3")
        out_made = sem("out_made")
        out_stored = sem("out_stored")

        block = ctx.enter_context(nc.Block())

        MAIN = E * PER_STEP

        def pair(s, j):
            if isinstance(s, int) and s == 0:
                return j
            if isinstance(s, int) and s == E:
                return PER_STEP * E - (PER_STEP - GU_PAIRS) + (j - GU_PAIRS)
            return s * PER_STEP + (j - (PER_STEP - GU_PAIRS))

        def slot_of(s0, j, ring):
            return pair(s0, j) % ring

        def parts(s0):
            return [j for j in range(PER_STEP) if (j < GU_PAIRS or s0 > 0) and (j >= GU_PAIRS or s0 < E)]

        def main_steps(eng, step):
            for s in range(3):
                step(s, s)
            with eng.Fori(0, (E - 4) // 2) as i:
                for u in (3, 4):
                    step(i * 2 + u, u)
            step(E - 1, E - 1)
            step(E, E)

        def overflow_blocks(eng, body):
            n = eng.value_load(n_over[0:1, 0:1], min_val=0, max_val=OVERFLOW)
            with eng.If(n):
                with eng.Fori(0, n) as v:
                    body(v)
            return n

        @block.sync
        def _(sp):
            for i in range(TILES):
                sp.dma_start(res[:, i, :], x_rows[i * P:(i + 1) * P, :]).then_inc(x_in[i], 16)

            def load(s, s0, j, e):
                q = slot_of(s0, j, RAW)
                src = gu_rows if j < GU_PAIRS else dn_rows
                c = j if j < GU_PAIRS else j - GU_PAIRS
                sp.dma_start(raw[:, q, :], src[bass.ds(e, 1), :, c * PAIR:(c + 1) * PAIR]
                             .rearrange("a p n -> (a p) n")).then_inc(raw_in[q], 16)

            def step(s, s0):
                for j in parts(s0):
                    if isinstance(s, int) and pair(s, j) == RAW - 3:
                        sp.wait_ge(pw_split, 1)
                    if not (isinstance(s, int) and pair(s, j) < RAW):
                        sp.wait_ge(lo_done, pair(s, j) - RAW + 1)
                    load(s, s0, j, s if j < GU_PAIRS else s - 1)

            main_steps(sp, step)

            sp.wait_ge(tables_made, 1)
            n = sp.value_load(n_over[0:1, 0:1], min_val=0, max_val=OVERFLOW)
            with sp.If(n):
                with sp.Fori(0, n) as v:
                    e = sp.value_load(over_e[0:1, bass.ds(v, 1)], min_val=0, max_val=E - 1)
                    for j in range(PER_STEP):
                        sp.wait_ge(lo_done, v * PER_STEP + (MAIN - PER_STEP + j + 1))
                        src = gu_rows if j < GU_PAIRS else dn_rows
                        c = j if j < GU_PAIRS else j - GU_PAIRS
                        sp.dma_start(raw[:, j, :], src[bass.ds(e, 1), :, c * PAIR:(c + 1) * PAIR]
                                     .rearrange("a p n -> (a p) n")).then_inc(raw_in[j], 16)
            sp.wait_ge(lo_done, n * PER_STEP + MAIN)
            sp.wait_ge(y_stored, n * 16 + 16 * E)
            by_choice = expert_out.rearrange("(k i p) d -> i p k d", k=K, p=P)
            for i in range(TILES):
                sp.dma_start(raw[:, i, :].rearrange("p (k d) -> p k d", k=K), by_choice[i])\
                    .then_inc(y_in[i], 16)
            for i in range(TILES):
                sp.wait_ge(out_made, i + 1)
                sp.dma_start(out_rows[i * P:(i + 1) * P, :], raw[:, i, 0:D]).then_inc(out_stored, 16)
            sp.wait_ge(out_stored, 16 * TILES)

        @block.gpsimd
        def _(pool):
            chain = [0]

            def link(ins):
                chain[0] += 1
                ins.then_inc(consts, 1)
                pool.wait_ge(consts, chain[0])

            nc.gpsimd.memset(eps[:], EPS)
            nc.gpsimd.memset(ident[:], 0.0)
            nc.gpsimd.memset(band_w[:], 1.0)
            nc.gpsimd.memset(halo_w[:], 1.0)
            link(nc.gpsimd.memset(tri_f[:], 1.0))
            nc.gpsimd.affine_select(out=ident[:], in_=ident[:], compare_op=ALU.not_equal, fill=1.0,
                                    base=0, pattern=[[-1, P]], channel_multiplier=1)
            nc.gpsimd.affine_select(out=tri_f[:], in_=tri_f[:], compare_op=ALU.is_gt, fill=0.0,
                                    base=0, pattern=[[1, P]], channel_multiplier=-1)
            link(nc.gpsimd.affine_select(out=band_w[:], in_=band_w[:], compare_op=ALU.is_ge, fill=0.0,
                                         base=0, pattern=[[0, NG], [1, P]], channel_multiplier=-1))
            for g, w in enumerate(WINDOWS):
                nc.gpsimd.affine_select(out=band_w[:, g, :], in_=band_w[:, g, :], compare_op=ALU.is_ge,
                                        fill=0.0, base=w - 1, pattern=[[-1, P]], channel_multiplier=1)
                nc.gpsimd.affine_select(out=halo_w[:, g, :], in_=halo_w[:, g, :], compare_op=ALU.is_ge,
                                        fill=0.0, base=w - 1 - P, pattern=[[-1, HALO]],
                                        channel_multiplier=1)
                nc.gpsimd.iota(count0[:, g:g + 1], [[0, 1]], base=1, channel_multiplier=1,
                               allow_small_or_imprecise_dtypes=True)
            nc.gpsimd.iota(iota_p[:], [[1, P]], base=0, channel_multiplier=0,
                           allow_small_or_imprecise_dtypes=True)
            nc.gpsimd.iota(iota_b[:], [[1, BLOCKS]], base=0, channel_multiplier=0,
                           allow_small_or_imprecise_dtypes=True)
            nc.gpsimd.iota(steps7[:], [[P, OVERFLOW // 2]], base=P, channel_multiplier=0,
                           allow_small_or_imprecise_dtypes=True)
            nc.gpsimd.iota(val[:], [[TOKENS, K], [P, TILES]], base=1, channel_multiplier=1,
                           allow_small_or_imprecise_dtypes=True)
            link(nc.gpsimd.memset(ones[:], 1.0))

            def store(i):
                pool.wait_ge(nx_made, i + 1)
                pool.dma_start(normed[i * P:(i + 1) * P, :], nx[:, i % 2, :, :].rearrange("p k t -> p (k t)"))\
                    .then_inc(nx_stored[i % 2], 16)

            for i in range(TILES):
                store(i)

            for par in range(2):
                pool.wait_ge(nx_stored[par], 16 * (TILES // 2))
            pool.wait_ge(nx_turned, TILES)
            nc.gpsimd.memset(xg[:], 0.0).then_inc(xg_clear, 1)
            pool.wait_ge(xg_clear, 1)
            pool.wait_ge(tables_made, 1)

            def last_row(s, rows):
                return rows - 1 if isinstance(s, int) else pool.snap((s | (rows - 1)) & (rows - 1))

            def gather(s, s0, copies):
                par = s0 % 2
                col = s if isinstance(s, int) else bass.ds(s, 1)
                nc.gpsimd.tensor_copy(src_now[:, par:par + 1],
                                      src_all[:, s:s + 1] if isinstance(s, int) else src_all[:, col])\
                    .then_inc(idx_now, 1)
                pool.wait_ge(idx_now, copies)
                pool.indirect_dma_start(
                    out=xg[:, par, :], out_offset=None, in_=normed[:, :],
                    in_offset=bass.IndirectOffsetOnAxis(ap=src_now[:, par:par + 1].bitcast(u32), axis=0),
                    bounds_check=last_row(s, TOKENS), oob_is_err=False).then_inc(gathered[par], 16)

            def scatter(s, copies):
                if not (isinstance(s, int) and s == 0):
                    pool.wait_ge(y_stored, s * 16)
                nc.gpsimd.tensor_copy(dst_now[:],
                                      dst_all[:, s:s + 1] if isinstance(s, int) else dst_all[:, bass.ds(s, 1)])\
                    .then_inc(idx_now, 1)
                pool.wait_ge(idx_now, copies)
                pool.wait_ge(y_copied, s + 1)
                pool.indirect_dma_start(
                    out=expert_out[:, :],
                    out_offset=bass.IndirectOffsetOnAxis(ap=dst_now[:].bitcast(u32), axis=0),
                    in_=ysb[:], in_offset=None,
                    bounds_check=last_row(s, K * TOKENS), oob_is_err=False).then_inc(y_stored, 16)

            gather(0, 0, 1)
            gather(1, 1, 2)

            def step(s, s0):
                if s0 == 0:
                    return
                if s0 < E - 1:
                    pool.wait_ge(x_turned, s)
                    gather(s + 1, s0 + 1, 2 * s + 1)
                scatter(s - 1, 2 * s + 2 if s0 < E - 1 else 2 * (E - 2) + 2 + (s0 - (E - 2)))

            main_steps(pool, step)

            n = pool.value_load(n_over[0:1, 0:1], min_val=0, max_val=OVERFLOW)
            with pool.If(n):
                with pool.Fori(0, n) as v:
                    pool.wait_ge(x_turned, v + E)
                    gather(v + E, 0, v * 2 + (2 * E + 1))
                    scatter(v + E, v * 2 + (2 * E + 2))

            pool.wait_ge(nfin_in, 16)
            for m in range(TILES):
                pool.wait_ge(scaled3, m + 1)
                nc.gpsimd.tensor_tensor(raw[:, m, 0:D], raw[:, m, D:2 * D], nf_all[:], ALU.mult)\
                    .then_inc(out_made, 1)

        @block.scalar
        def _(act):
            act.dma_start(nm_rows[:], norm_mix.rearrange("a (j p) -> (a j) p", p=P)).then_inc(mix_w_in, 16)
            act.dma_start(pw_in[:], pool_w[0].rearrange("g (j p) d -> p (g j) d", p=P)).then_inc(mix_w_in, 16)
            act.dma_start(sc_all[:], pool_scale.to_broadcast([P, D])).then_inc(mix_w_in, 16)
            act.dma_start(nf_all[:], norm_ffn.to_broadcast([P, D])).then_inc(nf_in, 16)
            act.dma_start(wr_g[:], w_rg[0].rearrange("(p k) e -> p (k e)", k=KD)).then_inc(router_w_in, 16)
            act.dma_start(wr_e[:], w_re[0].rearrange("(p k) e -> p (k e)", k=KD)).then_inc(router_w_in, 16)
            act.dma_start(bias[:, 0:NG], b_rg.to_broadcast([P, NG])).then_inc(router_w_in, 16)
            act.dma_start(bias[:, NG:NL], b_re.to_broadcast([P, E])).then_inc(router_w_in, 16)

            chain = [0]

            def root_mean_square(where, i, sums, roots):
                chain[0] += 1
                nc.scalar.activation(where, res[:, i, :], ACT.Square, accum_out=sums[:, i:i + 1])\
                    .then_inc(act_step, 1)
                act.wait_ge(act_step, chain[0])
                return nc.scalar.activation(roots[:, i:i + 1], sums[:, i:i + 1], ACT.Sqrt,
                                            scale=1.0 / D, bias=eps[:])

            def square(i):
                act.wait_ge(x_in[i], 16)
                root_mean_square(junk[:], i, ss, rs).then_inc(squares, 1)

            def split_x(i):
                act.wait_ge(scales, i + 1)
                if i >= 2:
                    act.wait_ge(pooled, i)
                nc.scalar.activation(xs_hi[:, i % 2, :], res[:, i, :], ACT.Identity,
                                     scale=rs[:, i:i + 1]).then_inc(xs_hi_done, 1)

            act.wait_ge(consts, 3)
            square(0)
            square(1)
            split_x(0)
            act.wait_ge(pw_made, 1)
            nc.scalar.activation(pw_hi[:], pw[:], ACT.Copy).then_inc(pw_hi_done, 1)
            for i in range(TILES + 1):
                if i < TILES:
                    act.wait_ge(pooled, i + 1)
                    if i >= 1:
                        act.wait_ge(mixed, i)
                    nc.scalar.activation(pt_hi[:].rearrange("p k t -> p (k t)"), PT, ACT.Copy)\
                        .then_inc(pt_hi_done, 1)
                if i + 2 < TILES:
                    square(i + 2)
                if i + 1 < TILES:
                    split_x(i + 1)
                if i >= 1:
                    m = i - 1
                    act.wait_ge(res_made, m + 1)
                    root_mean_square(junk[:], m, ss2, rs2).then_inc(squares2, 1)
                if i >= 2:
                    m = i - 2
                    act.wait_ge(nx_turned, m + 1)
                    if m >= 2:
                        act.wait_ge(logits_done, m - 1)
                    nc.scalar.activation(nxT[:, m % 2, :, :].rearrange("p k t -> p (k t)"), NXT, ACT.Copy)\
                        .then_inc(nxT_copied, 1)
            m = TILES - 1
            act.wait_ge(nx_turned, m + 1)
            act.wait_ge(logits_done, m - 1)
            nc.scalar.activation(nxT[:, m % 2, :, :].rearrange("p k t -> p (k t)"), NXT, ACT.Copy)\
                .then_inc(nxT_copied, 1)

            act.wait_ge(g_shift, 1)
            nc.scalar.activation(gexp[:], t32[0][:], ACT.Exp).then_inc(g_exp, 1)
            act.wait_ge(e_shift, 1)
            nc.scalar.activation(t8[3][:], t8[2][:], ACT.Exp).then_inc(e_exp, 1)

            def split_pair(s, s0, j, use):
                q = slot_of(s0, j, RAW)
                act.wait_ge(raw_in[q], use)
                if not (isinstance(s, int) and pair(s, j) < SPLIT):
                    act.wait_ge(pair_used, pair(s, j) - SPLIT + 1)
                nc.scalar.activation(w_hi[:, slot_of(s0, j, SPLIT), :], raw[:, q, :], ACT.Copy)\
                    .then_inc(hi_done, 1)

            def uses(s, s0, j):
                if isinstance(s, int):
                    return 16 * (pair(s, j) // RAW + 1)
                return (s - s0) * 8 + 16 * (pair(s0, j) // RAW + 1)

            def split_x_block(s):
                act.wait_ge(x_turned, s + 1)
                nc.scalar.activation(x_hi[:].rearrange("p k t -> p (k t)"), XT, ACT.Copy)\
                    .then_inc(x_hi_done, 1)

            def silu_block(s, gu_end):
                act.wait_ge(pair_used, gu_end)
                if not (isinstance(s, int) and s == 0):
                    act.wait_ge(hid_made, s)
                nc.scalar.activation(silu[:], GU[:, 0:F], ACT.Silu).then_inc(silu_done, 1)

            def split_h_block(s, dn_end):
                act.wait_ge(hid_turned, s + 1)
                if dn_end is not None:
                    act.wait_ge(pair_used, dn_end)
                nc.scalar.activation(h_hi[:].rearrange("p k t -> p (k t)"), HT, ACT.Copy)\
                    .then_inc(h_hi_done, 1)

            def copy_y(s, dn_end):
                act.wait_ge(pair_used, dn_end)
                if not (isinstance(s, int) and s == 0):
                    act.wait_ge(y_stored, s * 16)
                nc.scalar.activation(ysb[:], Y, ACT.Copy).then_inc(y_copied, 1)

            def step(s, s0):
                js = parts(s0)
                for j in js:
                    if s0 == 0 and j == 0:
                        act.wait_ge(tables_made, 1)
                    if s0 >= 1 and j == js[0]:
                        silu_block(s - 1, pair(s - 1, GU_PAIRS - 1) + 1 if s0 > 1 else GU_PAIRS)
                        if s0 < E:
                            split_x_block(s)
                    if s0 == 0 and j == SPLIT:
                        split_x_block(s)
                    if s0 >= 1 and j == (2 if s0 < E else PER_STEP - 1):
                        split_h_block(s - 1, None if s0 == 1 else pair(s - 1, PER_STEP - 1) + 1)
                    split_pair(s, s0, j, uses(s, s0, j))
                    if s0 >= 2 and j == (2 if s0 < E else PER_STEP - 1):
                        copy_y(s - 2, pair(s - 1, PER_STEP - 1) + 1)

            main_steps(act, step)
            copy_y(E - 1, MAIN)

            n = act.value_load(n_over[0:1, 0:1], min_val=0, max_val=OVERFLOW)
            with act.If(n):
                with act.Fori(0, n) as v:
                    first = v * PER_STEP + MAIN

                    def over_pair(j):
                        act.wait_ge(raw_in[j], v * 16 + 16 * (MAIN // RAW + 1))
                        act.wait_ge(pair_used, first + (j - SPLIT + 1))
                        nc.scalar.activation(w_hi[:, j % SPLIT, :], raw[:, j, :], ACT.Copy)\
                            .then_inc(hi_done, 1)

                    split_x_block(v + E)
                    for j in range(GU_PAIRS):
                        over_pair(j)
                    silu_block(v + E, first + GU_PAIRS)
                    split_h_block(v + E, first)
                    for j in range(GU_PAIRS, PER_STEP):
                        over_pair(j)
                    copy_y(v + E, first + PER_STEP)

            act.wait_ge(y_stored, n * 16 + 16 * E)
            act.dma_start(nf_all[:], norm_final.rearrange("(a d) -> a d", a=1).to_broadcast([P, D]))\
                .then_inc(nfin_in, 16)
            for i in range(TILES + 1):
                if i < TILES:
                    act.wait_ge(total_made, i + 1)
                    root_mean_square(raw[:, i, 0:D], i, ss, rs).then_inc(squares3, 1)
                if i >= 1:
                    act.wait_ge(scales3, i)
                    nc.scalar.activation(raw[:, i - 1, D:2 * D], res[:, i - 1, :], ACT.Identity,
                                         scale=rs[:, i - 1:i]).then_inc(scaled3, 1)

        @block.vector
        def _(dve):
            chain = [0]

            def link(ins):
                chain[0] += 1
                ins.then_inc(dve_step, 1)
                dve.wait_ge(dve_step, chain[0])

            V = nc.vector

            POOL_CONSTS = 3
            dve.wait_ge(consts, POOL_CONSTS)
            for g, w in enumerate(WINDOWS):
                last = V.tensor_scalar(count0[:, g:g + 1], count0[:, g:g + 1], float(w), None, ALU.min)
            link(last)
            V.tensor_scalar(ncount0[:], count0[:], -1.0, None, ALU.mult)
            link(V.reciprocal(fix0[:], count0[:]))
            for g, w in enumerate(WINDOWS):
                V.tensor_scalar(fix0[:, g:g + 1], fix0[:, g:g + 1], float(w), None, ALU.mult)
                V.scalar_tensor_tensor(band[:, g, :], ident[:], -float(w), band_w[:, g, :],
                                       ALU.mult, ALU.add)
                V.scalar_tensor_tensor(band0[:, g, :], ident[:], ncount0[:, g:g + 1], band_w[:, g, :],
                                       ALU.mult, ALU.add)
            V.tensor_copy(halo[:], halo_w[:])
            V.tensor_copy(tri[:], tri_f[:])

            def scale_x(i):
                dve.wait_ge(squares, i + 1)
                V.reciprocal(rs[:, i:i + 1], rs[:, i:i + 1]).then_inc(scales, 1)

            def x_low(i):
                dve.wait_ge(xs_hi_done, i + 1)
                V.scalar_tensor_tensor(xs_lo[:, i % 2, :], res[:, i, :], rs[:, i:i + 1],
                                       xs_hi[:, i % 2, :].bitcast(f32), ALU.mult, ALU.subtract)\
                    .then_inc(xs_split, 1)

            dve.wait_ge(mix_w_in, 48)
            dve.wait_ge(nm_turned, 1)
            for g, w in enumerate(WINDOWS):
                last = V.tensor_scalar(nm[:, 2 * g:2 * g + 2], MISC[:, 2 * g:2 * g + 2], 1.0 / w, None,
                                       ALU.mult)
            link(last)
            for c in range(KD):
                g = c // 2
                last = V.scalar_tensor_tensor(pw[:, c, :], pw_in[:, c, :], nm[:, c:c + 1],
                                              sc_all[:, g * 2 * P:(g + 1) * 2 * P], ALU.mult, ALU.mult)
            last.then_inc(pw_made, 1)
            scale_x(0)
            scale_x(1)
            x_low(0)
            dve.wait_ge(pw_hi_done, 1)
            link(V.tensor_tensor(pw_lo[:], pw[:], pw_hi[:].bitcast(f32), ALU.subtract))
            dve.wait_ge(router_w_in, 64)
            V.tensor_copy(wr[:, :, 0:NG], wr_g[:].rearrange("p (k e) -> p k e", k=KD))
            V.tensor_copy(wr[:, :, NG:NL], wr_e[:].rearrange("p (k e) -> p k e", k=KD)).then_inc(pw_split, 1)
            dve.wait_ge(nf_in, 16)

            def norm2(m):
                dve.wait_ge(squares2, m + 1)
                link(V.reciprocal(rs2[:, m:m + 1], rs2[:, m:m + 1]))
                if m >= 2:
                    dve.wait_ge(nx_stored[m % 2], 16 * (m // 2))
                    dve.wait_ge(nx_turned, m - 1)
                V.scalar_tensor_tensor(nx[:, m % 2, :, :].rearrange("t k p -> t p k"),
                                       res[:, m, :].rearrange("t (p k) -> t p k", k=KD),
                                       rs2[:, m:m + 1],
                                       nf_all[:].rearrange("t (p k) -> t p k", k=KD),
                                       ALU.mult, ALU.mult).then_inc(nx_made, 1)

            for i in range(TILES + 1):
                if i < TILES:
                    dve.wait_ge(pt_hi_done, i + 1)
                    V.tensor_tensor(pt_lo[:].rearrange("p k t -> p (k t)"), PT,
                                    pt_hi[:].rearrange("p k t -> p (k t)").bitcast(f32), ALU.subtract)\
                        .then_inc(pt_split, 1)
                if i + 2 < TILES:
                    scale_x(i + 2)
                if i + 1 < TILES:
                    x_low(i + 1)
                if i < TILES:
                    dve.wait_ge(mixed, i + 1)
                    if i == 0:
                        for g in range(NG):
                            c = slice(g * 2 * P, (g + 1) * 2 * P)
                            last = V.scalar_tensor_tensor(res[:, i, c], PY[:, c], fix0[:, g:g + 1],
                                                          res[:, i, c], ALU.mult, ALU.add)
                    else:
                        last = V.tensor_tensor(res[:, i, :], PY, res[:, i, :], ALU.add)
                    last.then_inc(res_made, 1)
                if i >= 1:
                    norm2(i - 1)

            def bc(ap, axis, shape):
                return ap.unsqueeze(axis).to_broadcast(shape)

            dve.wait_ge(logits_done, TILES)
            link(V.tensor_tensor(logit[:], LG[:, 0:TILES * NL].rearrange("p (i e) -> p i e", e=NL),
                                 bc(bias[:], 1, [P, TILES, NL]), ALU.add))
            gl = logit[:, :, 0:NG]
            el = logit[:, :, NG:NL].rearrange("p i (g j) -> p i g j", g=NG)
            S8, S4 = [P, TILES, NJ], [P, TILES, NG]

            def first_max(onehot, src, top, scratch, n, shape):
                link(V.tensor_reduce(top, src, AX, ALU.max))
                link(V.tensor_tensor(scratch, src, bc(top, 2, shape), ALU.is_lt))
                link(V.scalar_tensor_tensor(scratch, scratch, float(n), bc(iota_b[:, 0:n], 1, shape),
                                            ALU.mult, ALU.add))
                link(V.tensor_reduce(t8[7][:], scratch, AX, ALU.min))
                return V.tensor_tensor(onehot, scratch, bc(t8[7][:], 2, shape), ALU.is_equal)

            link(first_max(first_g[:], gl, t8[0][:], t32[1][:], NG, S4))
            V.tensor_tensor(t32[0][:], gl, bc(t8[0][:], 2, S4), ALU.subtract).then_inc(g_shift, 1)
            S48 = [P, TILES, NG, NJ]
            link(V.tensor_tensor(byg[:], el, bc(first_g[:], 3, S48), ALU.mult))
            link(V.tensor_reduce(t64[0][:], byg[:].rearrange("p i g j -> p i j g"), AX, ALU.add))
            link(first_max(t64[1][:], t64[0][:], t8[1][:], t64[3][:], NJ, S8))
            link(V.tensor_scalar(t64[4][:], t64[1][:], -3.0e38, None, ALU.mult))
            link(V.tensor_tensor(t64[4][:], t64[4][:], t64[0][:], ALU.add))
            link(first_max(t64[2][:], t64[4][:], t8[4][:], t64[3][:], NJ, S8))
            V.tensor_tensor(t8[2][:], t8[4][:], t8[1][:], ALU.subtract).then_inc(e_shift, 1)
            for k in range(K):
                last = V.tensor_tensor(pick[:, k, :, :].rearrange("p i (g j) -> p i g j", g=NG),
                                       bc(first_g[:], 3, S48), bc(t64[1 + k][:], 2, S48), ALU.mult)
            link(last)
            V.memset(chosen[:, TILES, :], 0.0)
            V.tensor_tensor(chosen[:, 0:TILES, :], pick[:, 0, :, :], pick[:, 1, :, :], ALU.add)\
                .then_inc(chosen_made, 1)
            dve.wait_ge(g_exp, 1)
            link(V.tensor_reduce(t8[5][:], gexp[:], AX, ALU.add))
            dve.wait_ge(e_exp, 1)
            link(V.scalar_tensor_tensor(t8[6][:], t8[3][:], 1.0, t8[5][:], ALU.add, ALU.mult))
            link(V.reciprocal(gate[:, 0, :], t8[6][:]))
            V.tensor_tensor(gate[:, 1, :], gate[:, 0, :], t8[3][:], ALU.mult)
            dve.wait_ge(ranked, 1)
            link(V.tensor_copy(rank[:].rearrange("p i e -> p (i e)"), MISC[:, 0:(TILES + 1) * E]))
            V.tensor_copy(rank_i[:], rank[:, 0:TILES, :])
            counts = rank[:, TILES, :]
            link(V.tensor_tensor(over[:], bc(counts, 2, [P, E, OVERFLOW // 2]),
                                 bc(steps7[:], 1, [P, E, OVERFLOW // 2]), ALU.is_gt))
            V.tensor_scalar(quot_i[:], rank_i[:], 7, None, ALU.logical_shift_right)
            V.tensor_scalar(rem_i[:], rank_i[:], P - 1, None, ALU.bitwise_and)
            link(V.tensor_reduce(e32[0][:], over[:], AX, ALU.add))
            V.tensor_copy(quot[:], quot_i[:])
            V.tensor_copy(rem[:], rem_i[:])
            a, b, shift = e32[0], e32[1], 1
            while shift < E:
                V.tensor_copy(b[:, 0:shift], a[:, 0:shift])
                link(V.tensor_tensor(b[:, shift:E], a[:, shift:E], a[:, 0:E - shift], ALU.add))
                a, b = b, (e32[2] if b is e32[1] else e32[1])
                shift *= 2
            ends = a
            V.tensor_copy(n_over[:], ends[:, E - 1:E])
            link(V.tensor_tensor(e32[3][:], ends[:], e32[0][:], ALU.subtract))
            link(V.scalar_tensor_tensor(e32[4][:], e32[3][:], float(E - 1), iota_b[:, 0:E],
                                        ALU.add, ALU.subtract))
            SE = [P, TILES, E]
            link(V.scalar_tensor_tensor(blk_of[:], quot[:], 0.0, bc(e32[4][:], 1, SE), ALU.is_gt, ALU.mult))
            link(V.tensor_tensor(blk_of[:], blk_of[:], quot[:], ALU.add))
            link(V.tensor_tensor(blk_of[:], blk_of[:], bc(iota_b[:, 0:E], 1, SE), ALU.add))
            SK = [P, K, TILES, E]
            link(V.tensor_tensor(prod[:], pick[:], bc(blk_of[:], 1, SK), ALU.mult))
            link(V.tensor_reduce(blk[:], prod[:], AX, ALU.add))
            link(V.tensor_tensor(prod[:], pick[:], bc(rem[:], 1, SK), ALU.mult))
            link(V.tensor_reduce(row[:], prod[:], AX, ALU.add))
            KT = K * TILES
            V.tensor_tensor(is_row[:], bc(iota_p[:], 1, [P, KT, P]),
                            bc(row[:].rearrange("p k i -> p (k i)"), 2, [P, KT, P]), ALU.is_equal)
            link(V.tensor_tensor(is_blk[:], bc(iota_b[:], 1, [P, KT, BLOCKS]),
                                 bc(blk[:].rearrange("p k i -> p (k i)"), 2, [P, KT, BLOCKS]), ALU.is_equal))
            V.tensor_tensor(is_val[:], is_blk[:],
                            bc(val[:].rearrange("p k i -> p (k i)"), 2, [P, KT, BLOCKS]), ALU.mult)\
                .then_inc(rows_made, 1)
            link(V.tensor_tensor(late[:], bc(ends[:], 1, [P, OVERFLOW + 1, E]),
                                 bc(iota_b[:, 0:OVERFLOW + 1], 2, [P, OVERFLOW + 1, E]), ALU.is_le))
            link(V.tensor_reduce(slot2[:, 0:OVERFLOW + 1], late[:], AX, ALU.add))
            link(V.tensor_scalar(slot2[:, 0:OVERFLOW + 1], slot2[:, 0:OVERFLOW + 1], float(E - 1), None, ALU.min))
            link(V.tensor_copy(over_e[:], slot2[:, 0:OVERFLOW + 1]))
            dve.wait_ge(slotted, 1)
            link(V.tensor_copy(slot[:], MISC[:, 0:BLOCKS]))
            link(V.tensor_scalar(slot2[:], slot[:], 0.0, FAR, ALU.is_equal, ALU.mult))
            link(V.tensor_tensor(slot[:], slot2[:], slot[:], ALU.add))
            V.tensor_scalar(dst_all[:], slot[:], -1.0, None, ALU.add)
            link(V.tensor_scalar(slot2[:], slot[:], float(TOKENS), -float(TOKENS), ALU.is_gt, ALU.mult))
            V.scalar_tensor_tensor(src_all[:], slot2[:], -1.0, slot[:], ALU.add, ALU.add)\
                .then_inc(tables_made, 1)

            def low_pair(s, s0, j):
                dve.wait_ge(hi_done, pair(s, j) + 1)
                q = slot_of(s0, j, SPLIT)
                V.tensor_tensor(w_lo[:, q, :], raw[:, slot_of(s0, j, RAW), :],
                                w_hi[:, q, :].bitcast(f32), ALU.subtract).then_inc(lo_done, 1)

            def low_x(s):
                dve.wait_ge(x_hi_done, s + 1)
                V.tensor_tensor(x_lo[:].rearrange("p k t -> p (k t)"), XT,
                                x_hi[:].rearrange("p k t -> p (k t)").bitcast(f32), ALU.subtract)\
                    .then_inc(x_split, 1)

            def hidden(s):
                dve.wait_ge(silu_done, s + 1)
                if not (isinstance(s, int) and s == 0):
                    dve.wait_ge(hid_turned, s)
                V.tensor_tensor(hid[:].rearrange("t k p -> t p k"),
                                silu[:].rearrange("t (p k) -> t p k", k=KF),
                                GU[:, F:2 * F].rearrange("t (p k) -> t p k", k=KF), ALU.mult)\
                    .then_inc(hid_made, 1)

            def low_h(s):
                dve.wait_ge(h_hi_done, s + 1)
                V.tensor_tensor(h_lo[:].rearrange("p k t -> p (k t)"), HT,
                                h_hi[:].rearrange("p k t -> p (k t)").bitcast(f32), ALU.subtract)\
                    .then_inc(h_split, 1)

            def step(s, s0):
                js = parts(s0)
                for j in js:
                    if s0 >= 1 and j == js[0]:
                        hidden(s - 1)
                        if s0 < E:
                            low_x(s)
                    if s0 == 0 and j == SPLIT:
                        low_x(s)
                    if s0 >= 1 and j == (2 if s0 < E else PER_STEP - 1):
                        low_h(s - 1)
                    low_pair(s, s0, j)

            main_steps(dve, step)

            n = dve.value_load(n_over[0:1, 0:1], min_val=0, max_val=OVERFLOW)
            with dve.If(n):
                with dve.Fori(0, n) as v:
                    def over_pair(j):
                        dve.wait_ge(hi_done, v * PER_STEP + (MAIN + j + 1))
                        V.tensor_tensor(w_lo[:, j % SPLIT, :], raw[:, j, :],
                                        w_hi[:, j % SPLIT, :].bitcast(f32), ALU.subtract)\
                            .then_inc(lo_done, 1)

                    low_x(v + E)
                    for j in range(GU_PAIRS):
                        over_pair(j)
                    hidden(v + E)
                    low_h(v + E)
                    for j in range(GU_PAIRS, PER_STEP):
                        over_pair(j)

            for i in range(TILES + 1):
                if i < TILES:
                    dve.wait_ge(y_in[i], 16)
                    for k in range(K):
                        last = V.scalar_tensor_tensor(res[:, i, :], raw[:, i, k * D:(k + 1) * D],
                                                      gate[:, k, i:i + 1], res[:, i, :],
                                                      ALU.mult, ALU.add)
                        if k < K - 1:
                            link(last)
                    last.then_inc(total_made, 1)
                if i >= 1:
                    dve.wait_ge(squares3, i)
                    V.reciprocal(rs[:, i - 1:i], rs[:, i - 1:i]).then_inc(scales3, 1)

        @block.tensor
        def _(pe):
            mm = nc.tensor.matmul

            pe.wait_ge(consts, 3)
            pe.wait_ge(mix_w_in, 48)
            nc.tensor.transpose(MISC[:, 0:KD], nm_rows[:], ident[0:KD, 0:KD]).then_inc(nm_turned, 1)

            def pool_tile(i):
                pe.wait_ge(xs_split, i + 1)
                if i >= 1:
                    pe.wait_ge(pt_split, i)
                for c in range(KD):
                    cols = slice(c * P, (c + 1) * P)
                    terms = [(xs, i % 2, (band if i else band0)[:, c // 2, :], c * P, P) for xs in (xs_hi, xs_lo)]
                    if i:
                        terms += [(xs, (i - 1) % 2, halo[:, c // 2, :], c * P, HALO) for xs in (xs_hi, xs_lo)]
                    for n, (xs, par, mask, c0, width) in enumerate(terms):
                        last = mm(PT[:, c0:c0 + width], xs[:, par, cols], mask,
                                  start=(n == 0), stop=(n == len(terms) - 1))
                last.then_inc(pooled, 1)

            def mix_tile(i):
                pe.wait_ge(pt_split, i + 1)
                if i == 0:
                    pe.wait_ge(pw_split, 1)
                if i >= 1:
                    pe.wait_ge(res_made, i)
                for g in range(NG):
                    terms = [(a, b, c) for c in (2 * g, 2 * g + 1)
                             for a, b in ((pt_hi, pw_hi), (pt_hi, pw_lo), (pt_lo, pw_hi))]
                    for n, (a, b, c) in enumerate(terms):
                        last = mm(PY[:, g * 2 * P:(g + 1) * 2 * P], a[:, c, :], b[:, c, :],
                                  start=(n == 0), stop=(n == len(terms) - 1))
                last.then_inc(mixed, 1)

            def turn_tile(i):
                pe.wait_ge(nx_made, i + 1)
                if i >= 1:
                    pe.wait_ge(nxT_copied, i)
                for c in range(KD):
                    last = nc.tensor.transpose(NXT[:, c * P:(c + 1) * P], nx[:, i % 2, c, :], ident[:])
                last.then_inc(nx_turned, 1)

            def logits_tile(i):
                pe.wait_ge(nxT_copied, i + 1)
                for c in range(KD):
                    last = mm(LG[:, i * NL:(i + 1) * NL], nxT[:, i % 2, c, :], wr[:, c, :],
                              start=(c == 0), stop=(c == KD - 1))
                last.then_inc(logits_done, 1)

            for i in range(TILES + 2):
                if i < TILES:
                    pool_tile(i)
                if i >= 2:
                    turn_tile(i - 2)
                if i >= 3:
                    logits_tile(i - 3)
                if i < TILES:
                    mix_tile(i)
            logits_tile(TILES - 1)

            pe.wait_ge(chosen_made, 1)
            pe.wait_ge(consts, 3)
            flat = chosen[:].rearrange("p i e -> p (i e)")
            mm(MISC[:, 0:(TILES + 1) * E], tri[:], flat, start=True, stop=False)
            for i in range(TILES):
                last = mm(MISC[:, (i + 1) * E:(TILES + 1) * E].rearrange("p (i e) -> p i e", e=E), ones[:],
                          chosen[:, i:i + 1, :].to_broadcast([P, TILES - i, E]),
                          start=False, stop=(i == TILES - 1))
            last.then_inc(ranked, 1)
            pe.wait_ge(rows_made, 1)
            for n in range(K * TILES):
                last = mm(MISC[:, 0:BLOCKS], is_row[:, n, :], is_val[:, n, :],
                          start=(n == 0), stop=(n == K * TILES - 1))
            last.then_inc(slotted, 1)

            def products(dst, hi, lo, j0, chunks, slot, cols=1024):
                for c in range(2):
                    ch = j0 + c
                    for a, b in ((hi, w_hi), (hi, w_lo), (lo, w_hi)):
                        for n in range(2):
                            last = mm(dst[:, n * N:(n + 1) * N], a[:, ch, :],
                                      b[:, slot, c * D + n * N:c * D + (n + 1) * N],
                                      start=(ch == 0 and a is hi and b is w_hi),
                                      stop=(ch == chunks - 1 and a is lo))
                return last

            def turn_x(s, s0, landed):
                pe.wait_ge(gathered[s0 % 2], landed)
                if not (isinstance(s, int) and s == 0):
                    pe.wait_ge(x_split, s)
                for c in range(KD):
                    last = nc.tensor.transpose(XT[:, c * P:(c + 1) * P],
                                               xg[:, s0 % 2, c * P:(c + 1) * P], ident[:])
                last.then_inc(x_turned, 1)

            def turn_h(s):
                pe.wait_ge(hid_made, s + 1)
                if not (isinstance(s, int) and s == 0):
                    pe.wait_ge(h_split, s)
                for c in range(KF):
                    last = nc.tensor.transpose(HT[:, c * P:(c + 1) * P], hid[:, c, :], ident[:])
                last.then_inc(hid_turned, 1)

            def gu_pair(s, j, q, slot):
                if j == 0:
                    pe.wait_ge(x_split, s + 1)
                    if not (isinstance(s, int) and s == 0):
                        pe.wait_ge(hid_made, s)
                pe.wait_ge(lo_done, q + 1)
                products(GU, x_hi, x_lo, 2 * j, KD, slot).then_inc(pair_used, 1)

            def dn_pair(s, j, q, slot):
                if j == 0:
                    pe.wait_ge(h_split, s + 1)
                    if not (isinstance(s, int) and s == 0):
                        pe.wait_ge(y_copied, s)
                pe.wait_ge(lo_done, q + 1)
                last = products(Y, h_hi, h_lo, 2 * j, KF, slot)
                last.then_inc(pair_used, 1)

            turn_x(0, 0, 16)

            def step(s, s0):
                for j in parts(s0):
                    q = slot_of(s0, j, SPLIT)
                    if j < GU_PAIRS:
                        gu_pair(s, j, pair(s, j), q)
                    if j == GU_PAIRS - 1 and s0 < E - 1:
                        landed = 16 * ((s + 1) // 2 + 1) if isinstance(s, int) else \
                            (s - s0) * 8 + 16 * ((s0 + 1) // 2 + 1)
                        turn_x(s + 1, s0 + 1, landed)
                    if j >= GU_PAIRS:
                        dn_pair(s - 1, j - GU_PAIRS, pair(s, j), q)
                if s0 < E:
                    turn_h(s)

            main_steps(pe, step)

            n = pe.value_load(n_over[0:1, 0:1], min_val=0, max_val=OVERFLOW)
            with pe.If(n):
                with pe.Fori(0, n) as v:
                    turn_x(v + E, 0, v * 16 + 16 * (E // 2 + 1))
                    for j in range(GU_PAIRS):
                        gu_pair(v + E, j, v * PER_STEP + (MAIN + j), j % SPLIT)
                    turn_h(v + E)
                    for j in range(GU_PAIRS, PER_STEP):
                        dn_pair(v + E, j - GU_PAIRS, v * PER_STEP + (MAIN + j), j % SPLIT)


_INS = ["x", "norm_mix", "norm_ffn", "norm_final", "pool_w", "pool_scale", "router_group_w",
        "router_group_b", "router_expert_w", "router_expert_b", "expert_w_gu", "expert_w_down"]


def kernel(**inputs):
    import concourse.bacc as _bacc
    from concourse.bass_utils import run_bass_kernel_spmd as _run

    nc = _bacc.Bacc("TRN2", target_bir_lowering=False, num_devices=1)
    arrays, args = {}, []
    for name in _INS:
        a = np.ascontiguousarray(inputs[name])
        arrays[f"in_{name}"] = a
        args.append(nc.dram_tensor(f"in_{name}", a.shape, mybir.dt.from_np(a.dtype), kind="ExternalInput").ap())
    out = nc.dram_tensor("out", inputs["x"].shape, mybir.dt.float32, kind="ExternalOutput").ap()
    hybrid_pool_moe(nc, *args, out)
    r = _run(nc, [arrays], core_ids=[0])
    return r.results[0]["out"]
```

```python
from contextlib import ExitStack

import numpy as np

import concourse.bass as bass
from concourse import mybir


def hybrid_pool_moe(nc, x, norm_mix, norm_ffn, norm_final, pool_w, pool_scale,
                    w_rg, b_rg, w_re, b_re, w_gu, w_down, out):
    f32, f32r, bf16 = mybir.dt.float32, mybir.dt.float32r, mybir.dt.bfloat16
    i32, u32 = mybir.dt.int32, mybir.dt.uint32
    ALU, ACT, AX = mybir.AluOpType, mybir.ActivationFunctionType, mybir.AxisListType.X

    P = 128
    TOKENS, D = x.shape[1], x.shape[2]
    TILES = TOKENS // P
    EPS = 1e-6
    WINDOWS = (2, 4, 8, 16)
    HALO = WINDOWS[-1]
    NG = w_rg.shape[2]
    E = w_re.shape[2]
    NJ = E // NG
    NL = NG + E
    K = 2
    F = w_down.shape[2]
    KD, KF = D // P, F // P
    N = 512
    OVERFLOW = K * TOKENS // P - 1
    BLOCKS = E + OVERFLOW + 1
    FAR = 100000.0
    PAIR = 2 * D
    PER_STEP = (KD + KF) // 2
    GU_PAIRS = KD // 2
    RAW, SPLIT, XG = 18, 3, 3
    FLIGHT = 4
    UNROLL = 3
    PEEL = 4

    gu_rows = w_gu[0].rearrange("e (p k) f -> e p (k f)", k=KD)
    dn_rows = w_down[0].rearrange("e (p k) d -> e p (k d)", k=KF)
    x_rows = x[0]
    out_rows = out[0]

    normed = nc.dram_tensor("normed", [TOKENS, D], f32).ap()
    total = nc.dram_tensor("total", [TOKENS, D], f32).ap()

    ctx = ExitStack()
    with ctx:
        def sem(name):
            return ctx.enter_context(nc.semaphore(name))

        KB = 1024
        ARENA = 204 * KB
        base = (nc.sbuf_base + 31) // 32 * 32
        ctx.enter_context(nc.sbuf_tensor("arena", [P, ARENA // 4], f32))

        def at(name, shape, dt, offset):
            return nc.alloc_sbuf_tensor_at(name, shape, dt, offset=base + offset)

        def small(name, shape, dt):
            return ctx.enter_context(nc.sbuf_tensor(name, shape, dt))

        SLOT = 4 * PAIR
        raw = [at(f"raw{q}", [P, PAIR], f32, q * SLOT) for q in range(RAW)]
        w_lo = [at(f"w_lo{q}", [P, PAIR], f32r, q * SLOT) for q in range(RAW)]
        HI = RAW * SLOT
        WORK = HI + SPLIT * SLOT
        NFIN = WORK + 32 * KB
        w_hi = at("w_hi", [P, SPLIT, PAIR], f32r, HI)
        nfin = at("nfin", [P, D], f32, NFIN)
        MIX_SLOT = RAW - 3
        RES_SLOT = MIX_SLOT - TILES // 2
        RW_SLOT = RES_SLOT - 3
        MIX, RES, RW = MIX_SLOT * SLOT, RES_SLOT * SLOT, RW_SLOT * SLOT
        res = at("res", [P, TILES, D], f32, RES)
        xg = at("xg", [P, XG, D], f32, WORK)
        x_hi = at("x_hi", [P, KD, P], f32r, WORK + 12 * KB)
        x_lo = at("x_lo", [P, KD, P], f32r, WORK + 16 * KB)
        silu = at("silu", [P, F], f32, WORK + 20 * KB)
        hid = at("hid", [P, KF, P], f32, WORK + 22 * KB)
        h_hi = at("h_hi", [P, KF, P], f32r, WORK + 24 * KB)
        h_lo = at("h_lo", [P, KF, P], f32r, WORK + 26 * KB)
        ysb = at("ysb", [P, D], f32, WORK + 28 * KB)
        XS = 3
        xs_hi = at("xs_hi", [P, XS, D], f32r, HI)
        xs_lo = at("xs_lo", [P, XS, D], f32r, HI + 12 * KB)
        pw_hi = at("pw_hi", [P, KD, 2 * P], f32r, MIX)
        pw_lo = at("pw_lo", [P, KD, 2 * P], f32r, MIX + 8 * KB)
        pt_hi = at("pt_hi", [P, KD, P], f32r, MIX + 16 * KB)
        pt_lo = at("pt_lo", [P, KD, P], f32r, MIX + 20 * KB)
        nx = at("nx", [P, 2, KD, P], f32, WORK)
        band0 = at("band0", [P, NG, P], f32r, WORK)
        nxT = at("nxT", [P, 2, KD, P], f32, WORK + 8 * KB)
        band = at("band", [P, NG, P], f32r, WORK + 16 * KB)
        halo = at("halo", [P, NG, HALO], f32r, WORK + 18 * KB)
        wr = at("wr", [P, KD, NL], f32, WORK + 18 * KB + 256)
        tri = at("tri", [P, P], bf16, WORK + 19 * KB + 384 + 128)
        ones = at("ones", [P, P], bf16, WORK + 19 * KB + 768)
        iota_p = at("iota_p", [P, P], bf16, WORK + 20 * KB)
        iota_b = at("iota_b", [P, BLOCKS], f32, WORK + 20 * KB + 256)
        tile_no = at("tile_no", [P, K * TILES], f32, WORK + 20 * KB + 448)
        part_no = at("part_no", [P, 1], f32, WORK + 20 * KB + 512)
        steps7 = at("steps7", [P, OVERFLOW // 2], f32, WORK + 20 * KB + 544)
        junk = at("junk", [P, D], bf16, WORK + 22 * KB)
        nf_all = at("nf_all", [P, D], f32, WORK + 24 * KB)
        pw_in = at("pw_in", [P, KD, 2 * P], f32, RW)
        pw = at("pw", [P, KD, 2 * P], f32, RW + 8 * KB)
        sc_all = at("sc_all", [P, D], f32, RW + 16 * KB)
        band_w = at("band_w", [P, NG, P], f32, RW + 20 * KB)
        halo_w = at("halo_w", [P, NG, HALO], f32, RW + 22 * KB)
        tri_f = at("tri_f", [P, P], f32, RW + 22 * KB + 256)
        nm_rows = at("nm_rows", [KD, P], f32, RW + 22 * KB + 768)
        wr_g = at("wr_g", [P, KD * NG], f32, WORK + 4 * KB)
        wr_e = at("wr_e", [P, KD * E], f32, WORK + 4 * KB + 128)
        cursor = [0, 0]

        def room(first, last):
            cursor[0], cursor[1] = first, last

        def tmp(name, shape, dt=f32):
            size = int(np.prod(shape)) * (2 if dt == bf16 else 4)
            here = cursor[0]
            cursor[0] += (size + 31) // 32 * 32
            assert cursor[0] <= cursor[1], name
            return at(name, [P] + list(shape), dt, here)

        KT = K * TILES
        room(WORK + 8 * KB, WORK + 16 * KB)
        pick = tmp("pick", [K, TILES, E])
        prod = tmp("prod", [K, TILES, E])
        part_of = tmp("part_of", [KT, BLOCKS], bf16)
        room(WORK + 28 * KB, WORK + 32 * KB)
        is_row = tmp("is_row", [KT, P], bf16)
        room(WORK + 24 * KB, WORK + 28 * KB)
        byg = tmp("byg", [TILES, NG, NJ])
        over = tmp("over", [E, OVERFLOW // 2])
        is_blk = tmp("is_blk", [KT, BLOCKS], bf16)
        room(WORK + 22 * KB, WORK + 24 * KB)
        t32 = [tmp(f"t32_{n}", [TILES, NG]) for n in range(2)]
        first_g = tmp("first_g", [TILES, NG])
        t64 = [tmp(f"t64_{n}", [TILES, NJ]) for n in range(5)]
        t8 = [tmp(f"t8_{n}", [TILES]) for n in range(8)]
        room(WORK + 20 * KB + 576, WORK + 22 * KB)
        chosen = tmp("chosen", [TILES + 1, E], bf16)
        PAD = E // 2
        run = [tmp(f"run{n}", [PAD + E]) for n in range(2)]
        e32 = [tmp(f"e32_{n}", [E]) for n in range(2)]
        room(WORK + 16 * KB, WORK + 18 * KB)
        tile_of = tmp("tile_of", [KT, BLOCKS], bf16)
        gate_of = [at(f"gate_of{n}", [P, KT, BLOCKS], bf16, where)
                   for n, where in enumerate((NFIN, NFIN + 1536, WORK + 24 * KB + 256))]
        late = at("late", [P, OVERFLOW + 1, E], f32, WORK + 16 * KB)
        late_n = at("late_n", [P, OVERFLOW + 1], f32, WORK + 24 * KB + 128)
        gexp = at("gexp", [P, TILES, NG], f32, WORK + 24 * KB)

        k16 = [small(f"k16_{n}", [P, KT], f32) for n in range(4)]
        k16i = [small(f"k16i_{n}", [P, KT], i32) for n in range(2)]
        row16 = small("row16", [P, KT], bf16)
        slot = [small(f"slot{n}", [P, BLOCKS], f32) for n in range(2)]
        ident = small("ident", [P, P], f32)
        logit = small("logit", [P, TILES, NL], f32)
        bias = small("bias", [P, NL], f32)
        ss = small("ss", [P, TILES], f32)
        rs = small("rs", [P, TILES], f32)
        ss2 = small("ss2", [P, TILES], f32)
        rs2 = small("rs2", [P, TILES], f32)
        count0 = small("count0", [P, NG], f32)
        ncount0 = small("ncount0", [P, NG], f32)
        fix0 = small("fix0", [P, NG], f32)
        eps = small("eps", [P, 1], f32)
        nm = small("nm", [P, KD], f32)
        gate = small("gate", [P, KT], f32)
        gate_rest = small("gate_rest", [P, 2, KT], f32)
        gate_part = small("gate_part", [P, 3, KT], bf16)
        gate_all = small("gate_all", [P, BLOCKS], f32)
        gate_now = small("gate_now", [P, 1], f32)
        src_all = small("src_all", [P, BLOCKS], i32)
        src_now = small("src_now", [P, XG], i32)
        dst_now = small("dst_now", [P, 1], i32)
        over_e = small("over_e", [P, OVERFLOW + 1], i32)
        n_over = small("n_over", [P, 1], i32)

        psum = ctx.enter_context(nc.psum_tensor("psum", [P, 8, N], f32))
        bank = lambda b, n=1: psum[:, b:b + n, :].rearrange("p b n -> p (b n)")
        PT, PY, NXT, LG, MISC, SLOTS = bank(0, 2), bank(2, 2), bank(4, 2), bank(6), bank(7), bank(6)
        GU, Y, XT, HT = bank(0, 2), bank(2, 2), bank(4, 2), bank(6)

        x_in = [sem(f"x_in{i}") for i in range(TILES)]
        nm_in = sem("nm_in")
        mix_w_in = sem("mix_w_in")
        router_w_in = sem("router_w_in")
        bias_in = sem("bias_in")
        nf_in = sem("nf_in")
        consts = sem("consts")
        dve_step = sem("dve_step")
        act_step = sem("act_step")
        nm_turned = sem("nm_turned")
        pw_made = sem("pw_made")
        pw_hi_done = sem("pw_hi_done")
        pw_split = sem("pw_split")
        squares = sem("squares")
        scales = sem("scales")
        xs_hi_done = sem("xs_hi_done")
        xs_split = sem("xs_split")
        pooled = sem("pooled")
        pt_hi_done = sem("pt_hi_done")
        pt_split = sem("pt_split")
        mixed = sem("mixed")
        res_made = sem("res_made")
        squares2 = sem("squares2")
        nx_made = sem("nx_made")
        nx_turned = sem("nx_turned")
        nxT_copied = sem("nxT_copied")
        nx_stored = [sem(f"nx_stored{i}") for i in range(2)]
        wr_made = sem("wr_made")
        logits_done = sem("logits_done")
        g_shift = sem("g_shift")
        g_exp = sem("g_exp")
        e_shift = sem("e_shift")
        e_exp = sem("e_exp")
        chosen_made = sem("chosen_made")
        ranked = sem("ranked")
        rows_made = sem("rows_made")
        is_blk_made = sem("is_blk_made")
        tile_of_made = sem("tile_of_made")
        slotted = sem("slotted")
        tables_made = sem("tables_made")
        gate_parts = sem("gate_parts")
        gate_of_made = sem("gate_of_made")
        gates_slotted = sem("gates_slotted")
        gates_made = sem("gates_made")
        res_stored = sem("res_stored")
        over_made = sem("over_made")
        raw_in = [sem(f"raw_in{i}") for i in range(RAW)]
        hi_done = sem("hi_done")
        lo_done = sem("lo_done")
        pair_used = sem("pair_used")
        idx_now = sem("idx_now")
        gathered = [sem(f"gathered{i}") for i in range(XG)]
        gate_put = sem("gate_put")
        xg_clear = sem("xg_clear")
        x_turned = sem("x_turned")
        x_hi_done = sem("x_hi_done")
        x_split = sem("x_split")
        silu_done = sem("silu_done")
        hid_made = sem("hid_made")
        hid_turned = sem("hid_turned")
        h_hi_done = sem("h_hi_done")
        h_split = sem("h_split")
        y_copied = sem("y_copied")
        y_stored = sem("y_stored")
        y_in = [sem(f"y_in{i}") for i in range(TILES)]
        nfin_in = sem("nfin_in")
        squares3 = sem("squares3")
        out_made = sem("out_made")
        out_stored = sem("out_stored")

        block = ctx.enter_context(nc.Block())

        MAIN = E * PER_STEP

        def pair(s, j):
            if isinstance(s, int) and s == 0:
                return j
            if isinstance(s, int) and s == E:
                return PER_STEP * E - (PER_STEP - GU_PAIRS) + (j - GU_PAIRS)
            return s * PER_STEP + (j - (PER_STEP - GU_PAIRS))

        def slot_of(s0, j, ring):
            return pair(s0, j) % ring

        def landed(q, turn):
            return turn * (16 * UNROLL * PER_STEP // RAW) + 16 * (q // RAW + 1)

        def parts(s0):
            return [j for j in range(PER_STEP) if (j < GU_PAIRS or s0 > 0) and (j >= GU_PAIRS or s0 < E)]

        def main_steps(eng, step, last=2):
            for s in range(PEEL):
                step(s, s, 0)
            with eng.Fori(0, (E + 1 - PEEL - last) // UNROLL) as i:
                for u in range(PEEL, PEEL + UNROLL):
                    step(i * UNROLL + u, u, i)
            for s in range(E + 1 - last, E + 1):
                step(s, s, 0)

        def overflow_blocks(eng, body):
            n = eng.value_load(n_over[0:1, 0:1], min_val=0, max_val=OVERFLOW)
            with eng.If(n):
                with eng.Fori(0, n) as v:
                    body(v)
            return n

        @block.sync
        def _(sp):
            def load_x(i):
                sp.dma_start(res[:, i, :], x_rows[i * P:(i + 1) * P, :]).then_inc(x_in[i], 16)

            load_x(0)
            sp.dma_start(nm_rows[:], norm_mix.rearrange("a (j p) -> (a j) p", p=P)).then_inc(nm_in, 16)
            load_x(1)
            sp.dma_start(pw_in[:], pool_w[0].rearrange("g (j p) d -> p (g j) d", p=P)).then_inc(mix_w_in, 16)
            sp.dma_start(sc_all[:], pool_scale.to_broadcast([P, D])).then_inc(mix_w_in, 16)
            load_x(2)
            sp.dma_start(nf_all[:], norm_ffn.to_broadcast([P, D])).then_inc(nf_in, 16)
            sp.dma_start(wr_g[:], w_rg[0].rearrange("(p k) e -> p (k e)", k=KD)).then_inc(router_w_in, 16)
            sp.dma_start(wr_e[:], w_re[0].rearrange("(p k) e -> p (k e)", k=KD)).then_inc(router_w_in, 16)
            for i in range(3, TILES):
                load_x(i)
            sp.dma_start(bias[:, 0:NG], b_rg.to_broadcast([P, NG])).then_inc(bias_in, 16)
            sp.dma_start(bias[:, NG:NL], b_re.to_broadcast([P, E])).then_inc(bias_in, 16)

            def load(s, s0, j, e):
                q = slot_of(s0, j, RAW)
                src = gu_rows if j < GU_PAIRS else dn_rows
                c = j if j < GU_PAIRS else j - GU_PAIRS
                sp.dma_start(raw[q][:], src[bass.ds(e, 1), :, c * PAIR:(c + 1) * PAIR]
                             .rearrange("a p n -> (a p) n")).then_inc(raw_in[q], 16)

            def step(s, s0, turn):
                for j in parts(s0):
                    if isinstance(s, int) and pair(s, j) == RW_SLOT:
                        sp.wait_ge(pw_split, 1)
                    if isinstance(s, int) and RES_SLOT <= pair(s, j) < MIX_SLOT:
                        for i in (2 * (pair(s, j) - RES_SLOT), 2 * (pair(s, j) - RES_SLOT) + 1):
                            sp.wait_ge(res_made, i + 1)
                            sp.dma_start(total[i * P:(i + 1) * P, :], res[:, i, :])\
                                .then_inc(res_stored, 16)
                        sp.wait_ge(nx_made, i + 1)
                        sp.wait_ge(res_stored, 16 * (i + 1))
                    if isinstance(s, int) and pair(s, j) == MIX_SLOT:
                        sp.wait_ge(mixed, TILES)
                    if not (isinstance(s, int) and pair(s, j) < RAW):
                        sp.wait_ge(pair_used, pair(s, j) - RAW + 1)
                    before = pair(s0, j) - FLIGHT
                    if before >= 0:
                        sp.wait_ge(raw_in[before % RAW], landed(before, turn))
                    load(s, s0, j, s if j < GU_PAIRS else s - 1)
                if s0 == PEEL - 1:
                    sp.wait_ge(gates_slotted, 1)
                    sp.dma_start(nfin[:], norm_final.rearrange("(a d) -> a d", a=1).to_broadcast([P, D]))\
                        .then_inc(nfin_in, 16)

            main_steps(sp, step)

            sp.wait_ge(over_made, 1)
            n = sp.value_load(n_over[0:1, 0:1], min_val=0, max_val=OVERFLOW)
            with sp.If(n):
                with sp.Fori(0, n) as v:
                    e = sp.value_load(over_e[0:1, bass.ds(v, 1)], min_val=0, max_val=E - 1)
                    for j in range(PER_STEP):
                        sp.wait_ge(pair_used, v * PER_STEP + (MAIN - PER_STEP + j + 1))
                        src = gu_rows if j < GU_PAIRS else dn_rows
                        c = j if j < GU_PAIRS else j - GU_PAIRS
                        sp.dma_start(raw[j][:], src[bass.ds(e, 1), :, c * PAIR:(c + 1) * PAIR]
                                     .rearrange("a p n -> (a p) n")).then_inc(raw_in[j], 16)
            sp.wait_ge(y_stored, n * 16 + 16 * E)
            for i in range(TILES):
                sp.dma_start(raw[i][:, 0:D], total[i * P:(i + 1) * P, :]).then_inc(y_in[i], 16)
            for i in range(TILES):
                sp.wait_ge(out_made, i + 1)
                sp.dma_start(out_rows[i * P:(i + 1) * P, :], raw[i][:, D:2 * D]).then_inc(out_stored, 16)
            sp.wait_ge(out_stored, 16 * TILES)

        @block.gpsimd
        def _(pool):
            chain = [0]

            def link(ins):
                chain[0] += 1
                ins.then_inc(consts, 1)
                pool.wait_ge(consts, chain[0])

            nc.gpsimd.memset(eps[:], EPS)
            nc.gpsimd.memset(ident[:], 0.0)
            nc.gpsimd.memset(band_w[:], 1.0)
            nc.gpsimd.memset(halo_w[:], 1.0)
            nc.gpsimd.iota(count0[:], [[0, NG]], base=1, channel_multiplier=1,
                           allow_small_or_imprecise_dtypes=True)
            link(nc.gpsimd.memset(tri_f[:], 1.0))
            nc.gpsimd.affine_select(out=ident[:], in_=ident[:], compare_op=ALU.not_equal, fill=1.0,
                                    base=0, pattern=[[-1, P]], channel_multiplier=1)
            link(nc.gpsimd.affine_select(out=band_w[:], in_=band_w[:], compare_op=ALU.is_ge, fill=0.0,
                                         base=0, pattern=[[0, NG], [1, P]], channel_multiplier=-1))
            for g, w in enumerate(WINDOWS):
                last = nc.gpsimd.affine_select(out=band_w[:, g, :], in_=band_w[:, g, :],
                                               compare_op=ALU.is_ge, fill=0.0, base=w - 1,
                                               pattern=[[-1, P]], channel_multiplier=1)
            link(last)
            for g, w in enumerate(WINDOWS):
                nc.gpsimd.affine_select(out=halo_w[:, g, :], in_=halo_w[:, g, :], compare_op=ALU.is_ge,
                                        fill=0.0, base=w - 1 - P, pattern=[[-1, HALO]],
                                        channel_multiplier=1)
            nc.gpsimd.affine_select(out=tri_f[:], in_=tri_f[:], compare_op=ALU.is_gt, fill=0.0,
                                    base=0, pattern=[[1, P]], channel_multiplier=-1)
            nc.gpsimd.iota(iota_p[:], [[1, P]], base=0, channel_multiplier=0,
                           allow_small_or_imprecise_dtypes=True)
            nc.gpsimd.iota(iota_b[:], [[1, BLOCKS]], base=0, channel_multiplier=0,
                           allow_small_or_imprecise_dtypes=True)
            nc.gpsimd.iota(tile_no[:], [[0, K], [P, TILES]], base=0, channel_multiplier=0,
                           allow_small_or_imprecise_dtypes=True)
            nc.gpsimd.iota(part_no[:], [[0, 1]], base=1, channel_multiplier=1,
                           allow_small_or_imprecise_dtypes=True)
            nc.gpsimd.iota(steps7[:], [[P, OVERFLOW // 2]], base=P, channel_multiplier=0,
                           allow_small_or_imprecise_dtypes=True)
            nc.gpsimd.memset(run[0][:], 0.0)
            nc.gpsimd.memset(run[1][:], 0.0)
            nc.gpsimd.memset(chosen[:], 0.0)
            link(nc.gpsimd.memset(ones[:], 1.0))

            def store(i):
                pool.wait_ge(nx_made, i + 1)
                pool.dma_start(normed[i * P:(i + 1) * P, :], nx[:, i % 2, :, :].rearrange("p k t -> p (k t)"))\
                    .then_inc(nx_stored[i % 2], 16)

            for i in range(TILES):
                store(i)

            for par in range(2):
                pool.wait_ge(nx_stored[par], 16 * (TILES // 2))
            pool.wait_ge(nx_turned, TILES)
            nc.gpsimd.memset(xg[:, 0:XG - 1, :], 0.0).then_inc(xg_clear, 1)
            pool.wait_ge(is_blk_made, 1)
            hot = [P, KT, BLOCKS]
            nc.gpsimd.tensor_tensor(tile_of[:], is_blk[:], tile_no[:].unsqueeze(2).to_broadcast(hot),
                                    ALU.mult).then_inc(tile_of_made, 1)
            nc.gpsimd.memset(xg[:, XG - 1, :], 0.0).then_inc(xg_clear, 1)
            pool.wait_ge(xg_clear, 2)
            pool.wait_ge(tables_made, 1)

            def last_row(s, more):
                return TOKENS - 1 if isinstance(s, int) else pool.snap((s | (more * TOKENS - 1)) & (TOKENS - 1))

            def column(s):
                return slice(s, s + 1) if isinstance(s, int) else bass.ds(s, 1)

            def gather(s, g, copies):
                nc.gpsimd.tensor_copy(src_now[:, g:g + 1], src_all[:, column(s)]).then_inc(idx_now, 1)
                pool.wait_ge(idx_now, copies)
                pool.indirect_dma_start(
                    out=xg[:, g, :], out_offset=None, in_=normed[:, :],
                    in_offset=bass.IndirectOffsetOnAxis(ap=src_now[:, g:g + 1].bitcast(u32), axis=0),
                    bounds_check=last_row(s, 1), oob_is_err=False).then_inc(gathered[g], 16)

            def scatter(s, copies):
                if isinstance(s, int) and s == 0:
                    pool.wait_ge(res_stored, 16 * TILES)
                    pool.wait_ge(gates_made, 1)
                else:
                    pool.wait_ge(y_stored, s * 16)
                nc.gpsimd.tensor_copy(gate_now[:], gate_all[:, column(s)]).then_inc(gate_put, 1)
                nc.gpsimd.tensor_copy(dst_now[:], src_all[:, column(s)]).then_inc(idx_now, 1)
                pool.wait_ge(idx_now, copies)
                pool.wait_ge(y_copied, s + 1)
                pool.indirect_dma_start(
                    out=total[:, :],
                    out_offset=bass.IndirectOffsetOnAxis(ap=dst_now[:].bitcast(u32), axis=0),
                    in_=ysb[:], in_offset=None,
                    bounds_check=last_row(s, 2), oob_is_err=False,
                    compute_op=ALU.add).then_inc(y_stored, 16)

            for s in range(XG):
                gather(s, s, s + 1)
            pool.wait_ge(gate_parts, 1)
            for n in range(3):
                last = nc.gpsimd.tensor_tensor(gate_of[n][:], is_blk[:],
                                               gate_part[:, n, :].unsqueeze(2).to_broadcast(hot), ALU.mult)
            last.then_inc(gate_of_made, 1)

            def step(s, s0, turn):
                if s0 < E - XG:
                    pool.wait_ge(x_turned, s + 1)
                    gather(s + XG, s0 % XG, s * 2 + (XG if s0 else XG + 1))
                if s0 > 0:
                    scatter(s - 1, s * 2 + XG + 1 if s0 < E - XG else E + s)

            main_steps(pool, step, 2 + UNROLL)

            pool.wait_ge(over_made, 1)
            n = pool.value_load(n_over[0:1, 0:1], min_val=0, max_val=OVERFLOW)
            with pool.If(n):
                with pool.Fori(0, n) as v:
                    pool.wait_ge(x_turned, v + E)
                    gather(v + E, 0, v * 2 + (2 * E + 1))
                    scatter(v + E, v * 2 + (2 * E + 2))

        @block.scalar
        def _(act):
            chain = [0]

            def root_mean_square(where, rows, i, sums, roots):
                chain[0] += 1
                nc.scalar.activation(where, rows, ACT.Square, accum_out=sums[:, i:i + 1])\
                    .then_inc(act_step, 1)
                act.wait_ge(act_step, chain[0])
                return nc.scalar.activation(roots[:, i:i + 1], sums[:, i:i + 1], ACT.Sqrt,
                                            scale=1.0 / D, bias=eps[:])

            def square(i):
                act.wait_ge(x_in[i], 16)
                root_mean_square(junk[:], res[:, i, :], i, ss, rs).then_inc(squares, 1)

            def split_x(i):
                act.wait_ge(scales, i + 1)
                if i >= XS:
                    act.wait_ge(pooled, i - XS + 2)
                nc.scalar.activation(xs_hi[:, i % XS, :], res[:, i, :], ACT.Identity,
                                     scale=rs[:, i:i + 1]).then_inc(xs_hi_done, 1)

            def split_pooled(i):
                act.wait_ge(pooled, i + 1)
                if i >= 1:
                    act.wait_ge(mixed, i)
                nc.scalar.activation(pt_hi[:].rearrange("p k t -> p (k t)"), PT, ACT.Copy)\
                    .then_inc(pt_hi_done, 1)

            def square_2(i):
                act.wait_ge(res_made, i + 1)
                root_mean_square(junk[:], res[:, i, :], i, ss2, rs2).then_inc(squares2, 1)

            def copy_turned(i):
                act.wait_ge(nx_turned, i + 1)
                if i >= 2:
                    act.wait_ge(logits_done, i - 1)
                nc.scalar.activation(nxT[:, i % 2, :, :].rearrange("p k t -> p (k t)"), NXT, ACT.Copy)\
                    .then_inc(nxT_copied, 1)

            act.wait_ge(consts, 1)
            square(0)
            split_x(0)
            square(1)
            act.wait_ge(pw_made, 1)
            nc.scalar.activation(pw_hi[:], pw[:], ACT.Copy).then_inc(pw_hi_done, 1)
            split_x(1)
            square(2)
            for i in range(TILES + 2):
                if i < TILES:
                    split_pooled(i)
                if 1 <= i <= TILES:
                    square_2(i - 1)
                if i + 2 < TILES:
                    split_x(i + 2)
                if i >= 2:
                    copy_turned(i - 2)
                if i + 3 < TILES:
                    square(i + 3)

            def router_exps():
                act.wait_ge(g_shift, 1)
                nc.scalar.activation(gexp[:], t32[0][:], ACT.Exp).then_inc(g_exp, 1)
                act.wait_ge(e_shift, 1)
                nc.scalar.activation(t8[3][:], t8[2][:], ACT.Exp).then_inc(e_exp, 1)

            def split_pair(s, s0, j, use):
                q = slot_of(s0, j, RAW)
                act.wait_ge(raw_in[q], use)
                if not (isinstance(s, int) and pair(s, j) < SPLIT):
                    act.wait_ge(pair_used, pair(s, j) - SPLIT + 1)
                nc.scalar.activation(w_hi[:, slot_of(s0, j, SPLIT), :], raw[q][:], ACT.Copy)\
                    .then_inc(hi_done, 1)

            def split_x_block(s):
                act.wait_ge(x_turned, s + 1)
                nc.scalar.activation(x_hi[:].rearrange("p k t -> p (k t)"), XT, ACT.Copy)\
                    .then_inc(x_hi_done, 1)

            def silu_block(s, gu_end):
                act.wait_ge(pair_used, gu_end)
                if not (isinstance(s, int) and s == 0):
                    act.wait_ge(hid_made, s)
                nc.scalar.activation(silu[:], GU[:, 0:F], ACT.Silu).then_inc(silu_done, 1)

            def split_h_block(s, dn_end):
                act.wait_ge(hid_turned, s + 1)
                if dn_end is not None:
                    act.wait_ge(pair_used, dn_end)
                nc.scalar.activation(h_hi[:].rearrange("p k t -> p (k t)"), HT, ACT.Copy)\
                    .then_inc(h_hi_done, 1)

            def copy_y(s, dn_end):
                act.wait_ge(pair_used, dn_end)
                if not (isinstance(s, int) and s == 0):
                    act.wait_ge(y_stored, s * 16)
                act.wait_ge(gate_put, s + 1)
                nc.scalar.activation(ysb[:], Y, ACT.Identity, scale=gate_now[:]).then_inc(y_copied, 1)

            def step(s, s0, turn):
                js = parts(s0)
                for j in js:
                    if s0 == 0 and j == 0:
                        act.wait_ge(mixed, TILES)
                    if s0 == 0 and j == 1:
                        router_exps()
                    if s0 >= 1 and j == js[0]:
                        silu_block(s - 1, pair(s - 1, GU_PAIRS - 1) + 1 if s0 > 1 else GU_PAIRS)
                        if s0 < E:
                            split_x_block(s)
                    if s0 == 0 and j == SPLIT:
                        split_x_block(s)
                    if s0 >= 1 and j == (2 if s0 < E else PER_STEP - 1):
                        split_h_block(s - 1, None if s0 == 1 else pair(s - 1, PER_STEP - 1) + 1)
                    split_pair(s, s0, j, landed(pair(s0, j), turn))
                    if s0 >= 2 and j == (2 if s0 < E else PER_STEP - 1):
                        copy_y(s - 2, pair(s - 1, PER_STEP - 1) + 1)

            main_steps(act, step)
            copy_y(E - 1, MAIN)

            act.wait_ge(over_made, 1)
            n = act.value_load(n_over[0:1, 0:1], min_val=0, max_val=OVERFLOW)
            with act.If(n):
                with act.Fori(0, n) as v:
                    first = v * PER_STEP + MAIN

                    def over_pair(j):
                        act.wait_ge(raw_in[j], v * 16 + 16 * ((MAIN - 1 - j) // RAW + 2))
                        act.wait_ge(pair_used, first + (j - SPLIT + 1))
                        nc.scalar.activation(w_hi[:, j % SPLIT, :], raw[j][:], ACT.Copy)\
                            .then_inc(hi_done, 1)

                    split_x_block(v + E)
                    for j in range(GU_PAIRS):
                        over_pair(j)
                    silu_block(v + E, first + GU_PAIRS)
                    split_h_block(v + E, first)
                    for j in range(GU_PAIRS, PER_STEP):
                        over_pair(j)
                    copy_y(v + E, first + PER_STEP)

            for i in range(TILES):
                act.wait_ge(y_in[i], 16)
                root_mean_square(junk[:], raw[i][:, 0:D], i, ss, rs).then_inc(squares3, 1)

        @block.vector
        def _(dve):
            chain = [0]

            def link(ins):
                chain[0] += 1
                ins.then_inc(dve_step, 1)
                dve.wait_ge(dve_step, chain[0])

            V = nc.vector

            def scale_x(i):
                dve.wait_ge(squares, i + 1)
                V.reciprocal(rs[:, i:i + 1], rs[:, i:i + 1]).then_inc(scales, 1)

            def x_low(i):
                dve.wait_ge(xs_hi_done, i + 1)
                V.scalar_tensor_tensor(xs_lo[:, i % XS, :], res[:, i, :], rs[:, i:i + 1],
                                       xs_hi[:, i % XS, :].bitcast(f32), ALU.mult, ALU.subtract)\
                    .then_inc(xs_split, 1)

            dve.wait_ge(consts, 3)
            for g, w in enumerate(WINDOWS):
                last = V.tensor_scalar(count0[:, g:g + 1], count0[:, g:g + 1], float(w), None, ALU.min)
            link(last)
            link(V.tensor_scalar(ncount0[:], count0[:], -1.0, None, ALU.mult))
            scale_x(0)
            for g, w in enumerate(WINDOWS):
                V.scalar_tensor_tensor(band0[:, g, :], ident[:], ncount0[:, g:g + 1], band_w[:, g, :],
                                       ALU.mult, ALU.add)
            x_low(0)
            dve.wait_ge(nm_turned, 1)
            for g, w in enumerate(WINDOWS):
                last = V.tensor_scalar(nm[:, 2 * g:2 * g + 2], MISC[:, 2 * g:2 * g + 2], 1.0 / w, None,
                                       ALU.mult)
            link(last)
            scale_x(1)
            dve.wait_ge(mix_w_in, 32)
            for c in range(KD):
                g = c // 2
                last = V.scalar_tensor_tensor(pw[:, c, :], pw_in[:, c, :], nm[:, c:c + 1],
                                              sc_all[:, g * 2 * P:(g + 1) * 2 * P], ALU.mult, ALU.mult)
            last.then_inc(pw_made, 1)
            dve.wait_ge(consts, 4)
            for g, w in enumerate(WINDOWS):
                V.scalar_tensor_tensor(band[:, g, :], ident[:], -float(w), band_w[:, g, :],
                                       ALU.mult, ALU.add)
            V.tensor_copy(halo[:], halo_w[:])
            V.tensor_copy(tri[:], tri_f[:])
            link(V.reciprocal(fix0[:], count0[:]))
            for g, w in enumerate(WINDOWS):
                V.tensor_scalar(fix0[:, g:g + 1], fix0[:, g:g + 1], float(w), None, ALU.mult)
            x_low(1)
            dve.wait_ge(pw_hi_done, 1)
            V.tensor_tensor(pw_lo[:], pw[:], pw_hi[:].bitcast(f32), ALU.subtract).then_inc(pw_split, 1)
            scale_x(2)

            def pooled_low(i):
                dve.wait_ge(pt_hi_done, i + 1)
                V.tensor_tensor(pt_lo[:].rearrange("p k t -> p (k t)"), PT,
                                pt_hi[:].rearrange("p k t -> p (k t)").bitcast(f32), ALU.subtract)\
                    .then_inc(pt_split, 1)

            def add_mixed(i):
                dve.wait_ge(mixed, i + 1)
                if i == 0:
                    for g in range(NG):
                        c = slice(g * 2 * P, (g + 1) * 2 * P)
                        last = V.scalar_tensor_tensor(res[:, i, c], PY[:, c], fix0[:, g:g + 1],
                                                      res[:, i, c], ALU.mult, ALU.add)
                else:
                    last = V.tensor_tensor(res[:, i, :], PY, res[:, i, :], ALU.add)
                last.then_inc(res_made, 1)

            def norm_2(m):
                dve.wait_ge(squares2, m + 1)
                link(V.reciprocal(rs2[:, m:m + 1], rs2[:, m:m + 1]))
                if m >= 2:
                    dve.wait_ge(nx_stored[m % 2], 16 * (m // 2))
                    dve.wait_ge(nx_turned, m - 1)
                V.scalar_tensor_tensor(nx[:, m % 2, :, :].rearrange("t k p -> t p k"),
                                       res[:, m, :].rearrange("t (p k) -> t p k", k=KD),
                                       rs2[:, m:m + 1],
                                       nf_all[:].rearrange("t (p k) -> t p k", k=KD),
                                       ALU.mult, ALU.mult).then_inc(nx_made, 1)

            for i in range(TILES + 1):
                if i >= 1:
                    add_mixed(i - 1)
                if i == 1:
                    dve.wait_ge(router_w_in, 32)
                    V.tensor_copy(wr[:, :, 0:NG], wr_g[:].rearrange("p (k e) -> p k e", k=KD))
                    V.tensor_copy(wr[:, :, NG:NL], wr_e[:].rearrange("p (k e) -> p k e", k=KD))\
                        .then_inc(wr_made, 1)
                    dve.wait_ge(nf_in, 16)
                if i < TILES:
                    pooled_low(i)
                if i >= 1:
                    norm_2(i - 1)
                if i + 2 < TILES:
                    x_low(i + 2)
                if i + 3 < TILES:
                    scale_x(i + 3)

            def low_first(j):
                dve.wait_ge(hi_done, j + 1)
                V.tensor_tensor(w_lo[j][:], raw[j][:], w_hi[:, j, :].bitcast(f32),
                                ALU.subtract).then_inc(lo_done, 1)

            def bc(ap, axis, shape):
                return ap.unsqueeze(axis).to_broadcast(shape)

            low_first(0)
            dve.wait_ge(logits_done, TILES)
            dve.wait_ge(bias_in, 32)
            link(V.tensor_tensor(logit[:], LG[:, 0:TILES * NL].rearrange("p (i e) -> p i e", e=NL),
                                 bc(bias[:], 1, [P, TILES, NL]), ALU.add))
            gl = logit[:, :, 0:NG]
            el = logit[:, :, NG:NL].rearrange("p i (g j) -> p i g j", g=NG)
            S8, S4 = [P, TILES, NJ], [P, TILES, NG]

            def first_max(onehot, src, top, scratch, n, shape):
                link(V.tensor_reduce(top, src, AX, ALU.max))
                link(V.tensor_tensor(scratch, src, bc(top, 2, shape), ALU.is_lt))
                link(V.scalar_tensor_tensor(scratch, scratch, float(n), bc(iota_b[:, 0:n], 1, shape),
                                            ALU.mult, ALU.add))
                link(V.tensor_reduce(t8[7][:], scratch, AX, ALU.min))
                return V.tensor_tensor(onehot, scratch, bc(t8[7][:], 2, shape), ALU.is_equal)

            link(first_max(first_g[:], gl, t8[0][:], t32[1][:], NG, S4))
            S48 = [P, TILES, NG, NJ]
            link(V.tensor_tensor(byg[:], el, bc(first_g[:], 3, S48), ALU.mult))
            link(V.tensor_reduce(t64[0][:], byg[:].rearrange("p i g j -> p i j g"), AX, ALU.add))
            link(first_max(t64[1][:], t64[0][:], t8[1][:], t64[3][:], NJ, S8))
            V.tensor_tensor(pick[:, 0, :, :].rearrange("p i (g j) -> p i g j", g=NG),
                            bc(first_g[:], 3, S48), bc(t64[1][:], 2, S48), ALU.mult)
            link(V.scalar_tensor_tensor(t64[4][:], t64[1][:], -3.0e38, t64[0][:], ALU.mult, ALU.add))
            link(first_max(t64[2][:], t64[4][:], t8[4][:], t64[3][:], NJ, S8))
            link(V.tensor_tensor(pick[:, 1, :, :].rearrange("p i (g j) -> p i g j", g=NG),
                                 bc(first_g[:], 3, S48), bc(t64[2][:], 2, S48), ALU.mult))
            V.tensor_tensor(chosen[:, 0:TILES, :], pick[:, 0, :, :], pick[:, 1, :, :], ALU.add)\
                .then_inc(chosen_made, 1)
            SK = [P, K, TILES, E]
            by_k = lambda ap: ap.rearrange("p (k i) -> p k i", k=K)
            link(V.tensor_tensor(prod[:], pick[:], iota_b[:, 0:E].unsqueeze(1).unsqueeze(1).to_broadcast(SK),
                                 ALU.mult))
            link(V.tensor_reduce(by_k(k16[0][:]), prod[:], AX, ALU.add))
            dve.wait_ge(ranked, 1)
            counts = MISC[:, TILES * E:(TILES + 1) * E]
            V.tensor_tensor(over[:], bc(counts, 2, [P, E, OVERFLOW // 2]),
                            bc(steps7[:], 1, [P, E, OVERFLOW // 2]), ALU.is_gt)
            link(V.tensor_tensor(prod[:], pick[:],
                                 MISC[:, 0:TILES * E].rearrange("p (i e) -> p i e", e=E).unsqueeze(1)
                                 .to_broadcast(SK), ALU.mult))
            V.tensor_reduce(by_k(k16[1][:]), prod[:], AX, ALU.add)
            link(V.tensor_reduce(run[0][:, PAD:], over[:], AX, ALU.add))
            V.tensor_copy(e32[0][:], run[0][:, PAD:])
            V.tensor_copy(k16i[0][:], k16[1][:])
            a, b, shift = run[0], run[1], 1
            while shift < E:
                link(V.tensor_tensor(b[:, PAD:], a[:, PAD:], a[:, PAD - shift:PAD + E - shift], ALU.add))
                a, b, shift = b, a, shift * 2
            ends = a[:, PAD:]
            V.tensor_scalar(k16i[1][:], k16i[0][:], P - 1, None, ALU.bitwise_and)
            link(V.tensor_tensor(e32[1][:], ends, e32[0][:], ALU.subtract))
            V.tensor_scalar(k16i[0][:], k16i[0][:], 7, None, ALU.logical_shift_right)
            link(V.scalar_tensor_tensor(e32[1][:], e32[1][:], float(E - 1), iota_b[:, 0:E],
                                        ALU.add, ALU.subtract))
            V.tensor_copy(row16[:], k16i[1][:])
            V.tensor_copy(k16[1][:], k16i[0][:])
            link(V.tensor_tensor(prod[:], pick[:], e32[1][:].unsqueeze(1).unsqueeze(1).to_broadcast(SK),
                                 ALU.mult))
            link(V.tensor_reduce(by_k(k16[2][:]), prod[:], AX, ALU.add))
            link(V.scalar_tensor_tensor(k16[3][:], k16[1][:], 0.0, k16[2][:], ALU.is_gt, ALU.mult))
            link(V.tensor_tensor(k16[3][:], k16[3][:], k16[1][:], ALU.add))
            link(V.tensor_tensor(k16[3][:], k16[3][:], k16[0][:], ALU.add))
            V.tensor_tensor(is_blk[:], bc(iota_b[:], 1, [P, KT, BLOCKS]), bc(k16[3][:], 2, [P, KT, BLOCKS]),
                            ALU.is_equal).then_inc(is_blk_made, 1)
            V.tensor_tensor(is_row[:], bc(iota_p[:], 1, [P, KT, P]), bc(row16[:], 2, [P, KT, P]),
                            ALU.is_equal)
            dve.wait_ge(is_blk_made, 1)
            V.tensor_scalar(part_of[:], is_blk[:], part_no[:], None, ALU.mult).then_inc(rows_made, 1)
            V.tensor_copy(n_over[:], ends[:, E - 1:E])
            dve.wait_ge(slotted, 1)
            link(V.tensor_copy(slot[0][:], SLOTS[:, 0:BLOCKS]))
            link(V.tensor_scalar(slot[1][:], slot[0][:], 0.0, FAR, ALU.is_equal, ALU.mult))
            V.scalar_tensor_tensor(src_all[:], slot[1][:], -1.0, slot[0][:], ALU.add, ALU.add)\
                .then_inc(tables_made, 1)
            V.tensor_tensor(t32[0][:], gl, bc(t8[0][:], 2, S4), ALU.subtract).then_inc(g_shift, 1)
            V.tensor_tensor(t8[2][:], t8[4][:], t8[1][:], ALU.subtract).then_inc(e_shift, 1)
            link(V.tensor_tensor(late[:], bc(ends, 1, [P, OVERFLOW + 1, E]),
                                 bc(iota_b[:, 0:OVERFLOW + 1], 2, [P, OVERFLOW + 1, E]), ALU.is_le))
            link(V.tensor_reduce(late_n[:], late[:], AX, ALU.add))
            V.tensor_scalar(over_e[:], late_n[:], float(E - 1), None, ALU.min).then_inc(over_made, 1)
            dve.wait_ge(g_exp, 1)
            link(V.tensor_reduce(t8[5][:], gexp[:], AX, ALU.add))
            dve.wait_ge(e_exp, 1)
            link(V.scalar_tensor_tensor(t8[6][:], t8[3][:], 1.0, t8[5][:], ALU.add, ALU.mult))
            link(V.reciprocal(gate[:, 0:TILES], t8[6][:]))
            link(V.tensor_tensor(gate[:, TILES:KT], gate[:, 0:TILES], t8[3][:], ALU.mult))
            left = gate[:]
            for n in range(3):
                last = V.tensor_copy(gate_part[:, n, :], left)
                if n < 2:
                    link(last)
                    link(V.tensor_tensor(gate_rest[:, n, :], left, gate_part[:, n, :], ALU.subtract))
                    left = gate_rest[:, n, :]
            last.then_inc(gate_parts, 1)
            low_first(1)
            low_first(2)

            def low_pair(s, s0, j):
                dve.wait_ge(hi_done, pair(s, j) + 1)
                q = slot_of(s0, j, SPLIT)
                V.tensor_tensor(w_lo[slot_of(s0, j, RAW)][:], raw[slot_of(s0, j, RAW)][:],
                                w_hi[:, q, :].bitcast(f32), ALU.subtract).then_inc(lo_done, 1)

            def low_x(s):
                dve.wait_ge(x_hi_done, s + 1)
                V.tensor_tensor(x_lo[:].rearrange("p k t -> p (k t)"), XT,
                                x_hi[:].rearrange("p k t -> p (k t)").bitcast(f32), ALU.subtract)\
                    .then_inc(x_split, 1)

            def hidden(s):
                dve.wait_ge(silu_done, s + 1)
                if not (isinstance(s, int) and s == 0):
                    dve.wait_ge(hid_turned, s)
                V.tensor_tensor(hid[:].rearrange("t k p -> t p k"),
                                silu[:].rearrange("t (p k) -> t p k", k=KF),
                                GU[:, F:2 * F].rearrange("t (p k) -> t p k", k=KF), ALU.mult)\
                    .then_inc(hid_made, 1)

            def low_h(s):
                dve.wait_ge(h_hi_done, s + 1)
                V.tensor_tensor(h_lo[:].rearrange("p k t -> p (k t)"), HT,
                                h_hi[:].rearrange("p k t -> p (k t)").bitcast(f32), ALU.subtract)\
                    .then_inc(h_split, 1)

            def step(s, s0, turn):
                js = parts(s0)
                for j in js:
                    if s0 >= 1 and j == js[0]:
                        hidden(s - 1)
                        if s0 < E:
                            low_x(s)
                    if s0 == 0 and j == SPLIT:
                        low_x(s)
                    if s0 == 1 and j == 0:
                        dve.wait_ge(gates_slotted, 1)
                        V.tensor_copy(gate_all[:], MISC[:, 0:BLOCKS]).then_inc(gates_made, 1)
                    if s0 >= 1 and j == (2 if s0 < E else PER_STEP - 1):
                        low_h(s - 1)
                    if s0 > 0 or j >= SPLIT:
                        low_pair(s, s0, j)

            main_steps(dve, step)

            dve.wait_ge(over_made, 1)
            n = dve.value_load(n_over[0:1, 0:1], min_val=0, max_val=OVERFLOW)
            with dve.If(n):
                with dve.Fori(0, n) as v:
                    def over_pair(j):
                        dve.wait_ge(hi_done, v * PER_STEP + (MAIN + j + 1))
                        V.tensor_tensor(w_lo[j][:], raw[j][:],
                                        w_hi[:, j % SPLIT, :].bitcast(f32), ALU.subtract)\
                            .then_inc(lo_done, 1)

                    low_x(v + E)
                    for j in range(GU_PAIRS):
                        over_pair(j)
                    hidden(v + E)
                    low_h(v + E)
                    for j in range(GU_PAIRS, PER_STEP):
                        over_pair(j)

            dve.wait_ge(nfin_in, 16)
            for i in range(TILES):
                dve.wait_ge(squares3, i + 1)
                link(V.reciprocal(rs[:, i:i + 1], rs[:, i:i + 1]))
                V.scalar_tensor_tensor(raw[i][:, D:2 * D], raw[i][:, 0:D], rs[:, i:i + 1], nfin[:],
                                       ALU.mult, ALU.mult).then_inc(out_made, 1)

        @block.tensor
        def _(pe):
            mm = nc.tensor.matmul

            pe.wait_ge(consts, 2)
            pe.wait_ge(nm_in, 16)
            nc.tensor.transpose(MISC[:, 0:KD], nm_rows[:], ident[0:KD, 0:KD]).then_inc(nm_turned, 1)

            def pool_tile(i):
                pe.wait_ge(xs_split, i + 1)
                if i >= 1:
                    pe.wait_ge(pt_split, i)
                if i == 1:
                    pe.wait_ge(pw_split, 1)
                for c in range(KD):
                    cols = slice(c * P, (c + 1) * P)
                    terms = [(xs, i % XS, (band if i else band0)[:, c // 2, :], c * P, P) for xs in (xs_hi, xs_lo)]
                    if i:
                        terms += [(xs, (i - 1) % XS, halo[:, c // 2, :], c * P, HALO) for xs in (xs_hi, xs_lo)]
                    for n, (xs, par, mask, c0, width) in enumerate(terms):
                        last = mm(PT[:, c0:c0 + width], xs[:, par, cols], mask,
                                  start=(n == 0), stop=(n == len(terms) - 1))
                last.then_inc(pooled, 1)

            def mix_tile(i):
                pe.wait_ge(pt_split, i + 1)
                if i == 0:
                    pe.wait_ge(pw_split, 1)
                if i >= 1:
                    pe.wait_ge(res_made, i)
                for g in range(NG):
                    terms = [(a, b, c) for c in (2 * g, 2 * g + 1)
                             for a, b in ((pt_hi, pw_hi), (pt_hi, pw_lo), (pt_lo, pw_hi))]
                    for n, (a, b, c) in enumerate(terms):
                        last = mm(PY[:, g * 2 * P:(g + 1) * 2 * P], a[:, c, :], b[:, c, :],
                                  start=(n == 0), stop=(n == len(terms) - 1))
                last.then_inc(mixed, 1)

            def turn_tile(i):
                pe.wait_ge(nx_made, i + 1)
                if i >= 1:
                    pe.wait_ge(nxT_copied, i)
                for c in range(KD):
                    last = nc.tensor.transpose(NXT[:, c * P:(c + 1) * P], nx[:, i % 2, c, :], ident[:])
                last.then_inc(nx_turned, 1)

            def logits_tile(i):
                pe.wait_ge(nxT_copied, i + 1)
                if i == 0:
                    pe.wait_ge(wr_made, 1)
                for c in range(KD):
                    last = mm(LG[:, i * NL:(i + 1) * NL], nxT[:, i % 2, c, :], wr[:, c, :],
                              start=(c == 0), stop=(c == KD - 1))
                last.then_inc(logits_done, 1)

            for i in range(TILES + 2):
                if i < TILES:
                    pool_tile(i)
                if i >= 2:
                    turn_tile(i - 2)
                if i >= 3:
                    logits_tile(i - 3)
                if i < TILES:
                    mix_tile(i)
            logits_tile(TILES - 1)

            pe.wait_ge(chosen_made, 1)
            pe.wait_ge(consts, 4)
            flat = chosen[:].rearrange("p i e -> p (i e)")
            mm(MISC[:, 0:(TILES + 1) * E], tri[:], flat, start=True, stop=False)
            for i in range(TILES):
                last = mm(MISC[:, (i + 1) * E:(TILES + 1) * E].rearrange("p (i e) -> p i e", e=E), ones[:],
                          chosen[:, i:i + 1, :].to_broadcast([P, TILES - i, E]),
                          start=False, stop=(i == TILES - 1))
            last.then_inc(ranked, 1)
            pe.wait_ge(rows_made, 1)
            pe.wait_ge(tile_of_made, 1)
            for n in range(KT):
                for hot in (part_of, tile_of):
                    last = mm(SLOTS[:, 0:BLOCKS], is_row[:, n, :], hot[:, n, :],
                              start=(n == 0 and hot is part_of), stop=(n == KT - 1 and hot is tile_of))
            last.then_inc(slotted, 1)

            def products(dst, hi, lo, j0, chunks, slot, raw_slot):
                for c in range(2):
                    ch = j0 + c
                    b_hi, b_lo = w_hi[:, slot, :], w_lo[raw_slot][:]
                    for a, b in ((hi, b_hi), (hi, b_lo), (lo, b_hi)):
                        for n in range(2):
                            last = mm(dst[:, n * N:(n + 1) * N], a[:, ch, :],
                                      b[:, c * D + n * N:c * D + (n + 1) * N],
                                      start=(ch == 0 and a is hi and b is b_hi),
                                      stop=(ch == chunks - 1 and a is lo))
                return last

            def slot_gates():
                pe.wait_ge(gate_of_made, 1)
                for n in range(KT):
                    for m in range(3):
                        last = mm(MISC[:, 0:BLOCKS], is_row[:, n, :], gate_of[m][:, n, :],
                                  start=(n == 0 and m == 0), stop=(n == KT - 1 and m == 2))
                last.then_inc(gates_slotted, 1)

            def turn_x(s, g, landed):
                pe.wait_ge(gathered[g], landed)
                if not (isinstance(s, int) and s == 0):
                    pe.wait_ge(x_split, s)
                for c in range(KD):
                    last = nc.tensor.transpose(XT[:, c * P:(c + 1) * P],
                                               xg[:, g, c * P:(c + 1) * P], ident[:])
                last.then_inc(x_turned, 1)

            def turn_h(s):
                pe.wait_ge(hid_made, s + 1)
                if not (isinstance(s, int) and s == 0):
                    pe.wait_ge(h_split, s)
                for c in range(KF):
                    last = nc.tensor.transpose(HT[:, c * P:(c + 1) * P], hid[:, c, :], ident[:])
                last.then_inc(hid_turned, 1)

            def gu_pair(s, j, q, slot, raw_slot):
                if j == 0:
                    pe.wait_ge(x_split, s + 1)
                    if not (isinstance(s, int) and s == 0):
                        pe.wait_ge(hid_made, s)
                pe.wait_ge(lo_done, q + 1)
                products(GU, x_hi, x_lo, 2 * j, KD, slot, raw_slot).then_inc(pair_used, 1)

            def dn_pair(s, j, q, slot, raw_slot):
                if j == 0:
                    pe.wait_ge(h_split, s + 1)
                    if not (isinstance(s, int) and s == 0):
                        pe.wait_ge(y_copied, s)
                pe.wait_ge(lo_done, q + 1)
                products(Y, h_hi, h_lo, 2 * j, KF, slot, raw_slot).then_inc(pair_used, 1)

            turn_x(0, 0, 16)

            def step(s, s0, turn):
                for j in parts(s0):
                    q, r = slot_of(s0, j, SPLIT), slot_of(s0, j, RAW)
                    if j < GU_PAIRS:
                        gu_pair(s, j, pair(s, j), q, r)
                    if s0 == 0 and j == 1:
                        slot_gates()
                    if j == GU_PAIRS - 1 and s0 < E - 1:
                        turn_x(s + 1, (s0 + 1) % XG, turn * 16 + 16 * ((s0 + 1) // XG + 1))
                    if j >= GU_PAIRS:
                        dn_pair(s - 1, j - GU_PAIRS, pair(s, j), q, r)
                if s0 < E:
                    turn_h(s)

            main_steps(pe, step)

            pe.wait_ge(over_made, 1)
            n = pe.value_load(n_over[0:1, 0:1], min_val=0, max_val=OVERFLOW)
            with pe.If(n):
                with pe.Fori(0, n) as v:
                    turn_x(v + E, 0, v * 16 + 16 * ((E - 1) // XG + 2))
                    for j in range(GU_PAIRS):
                        gu_pair(v + E, j, v * PER_STEP + (MAIN + j), j % SPLIT, j)
                    turn_h(v + E)
                    for j in range(GU_PAIRS, PER_STEP):
                        dn_pair(v + E, j - GU_PAIRS, v * PER_STEP + (MAIN + j), j % SPLIT, j)


_INS = ["x", "norm_mix", "norm_ffn", "norm_final", "pool_w", "pool_scale", "router_group_w",
        "router_group_b", "router_expert_w", "router_expert_b", "expert_w_gu", "expert_w_down"]


def kernel(**inputs):
    import concourse.bacc as _bacc
    from concourse.bass_utils import run_bass_kernel_spmd as _run

    nc = _bacc.Bacc("TRN2", target_bir_lowering=False, num_devices=1)
    arrays, args = {}, []
    for name in _INS:
        a = np.ascontiguousarray(inputs[name])
        arrays[f"in_{name}"] = a
        args.append(nc.dram_tensor(f"in_{name}", a.shape, mybir.dt.from_np(a.dtype), kind="ExternalInput").ap())
    out = nc.dram_tensor("out", inputs["x"].shape, mybir.dt.float32, kind="ExternalOutput").ap()
    hybrid_pool_moe(nc, *args, out)
    r = _run(nc, [arrays], core_ids=[0])
    return r.results[0]["out"]
```

```python
from contextlib import ExitStack

import numpy as np

import concourse.bass as bass
from concourse import mybir


def hybrid_pool_moe(nc, x, norm_mix, norm_ffn, norm_final, pool_w, pool_scale,
                    w_rg, b_rg, w_re, b_re, w_gu, w_down, out):
    f32, f32r, bf16 = mybir.dt.float32, mybir.dt.float32r, mybir.dt.bfloat16
    i32, u32 = mybir.dt.int32, mybir.dt.uint32
    ALU, ACT, AX = mybir.AluOpType, mybir.ActivationFunctionType, mybir.AxisListType.X

    P = 128
    TOKENS, D = x.shape[1], x.shape[2]
    TILES = TOKENS // P
    EPS = 1e-6
    WINDOWS = (2, 4, 8, 16)
    HALO = WINDOWS[-1]
    NG = w_rg.shape[2]
    E = w_re.shape[2]
    NJ = E // NG
    NL = NG + E
    K = 2
    F = w_down.shape[2]
    KD, KF = D // P, F // P
    N = 512
    OVERFLOW = K * TOKENS // P - 1
    BLOCKS = E + OVERFLOW + 1
    FAR = 100000.0
    PAIR = 2 * D
    PER_STEP = (KD + KF) // 2
    GU_PAIRS = KD // 2
    RAW, SPLIT, XG = 18, 3, 3
    FLIGHT = 4
    UNROLL = 3
    PEEL = 4

    gu_rows = w_gu[0].rearrange("e (p k) f -> e p (k f)", k=KD)
    dn_rows = w_down[0].rearrange("e (p k) d -> e p (k d)", k=KF)
    x_rows = x[0]
    out_rows = out[0]

    normed = nc.dram_tensor("normed", [TOKENS, D], f32).ap()
    total = nc.dram_tensor("total", [TOKENS, D], f32).ap()

    ctx = ExitStack()
    with ctx:
        def sem(name):
            return ctx.enter_context(nc.semaphore(name))

        KB = 1024
        ARENA = 204 * KB
        base = (nc.sbuf_base + 31) // 32 * 32
        ctx.enter_context(nc.sbuf_tensor("arena", [P, ARENA // 4], f32))

        def at(name, shape, dt, offset):
            return nc.alloc_sbuf_tensor_at(name, shape, dt, offset=base + offset)

        def small(name, shape, dt):
            return ctx.enter_context(nc.sbuf_tensor(name, shape, dt))

        SLOT = 4 * PAIR
        raw = [at(f"raw{q}", [P, PAIR], f32, q * SLOT) for q in range(RAW)]
        w_lo = [at(f"w_lo{q}", [P, PAIR], f32r, q * SLOT) for q in range(RAW)]
        HI = RAW * SLOT
        WORK = HI + SPLIT * SLOT
        NFIN = WORK + 32 * KB
        w_hi = at("w_hi", [P, SPLIT, PAIR], f32r, HI)
        nfin = at("nfin", [P, D], f32, NFIN)
        MIX_SLOT = RAW - 3
        RES_SLOT = MIX_SLOT - TILES // 2
        RW_SLOT = RES_SLOT - 3
        MIX, RES, RW = MIX_SLOT * SLOT, RES_SLOT * SLOT, RW_SLOT * SLOT
        res = at("res", [P, TILES, D], f32, RES)
        xg = at("xg", [P, XG, D], f32, WORK)
        x_hi = at("x_hi", [P, KD, P], f32r, WORK + 12 * KB)
        x_lo = at("x_lo", [P, KD, P], f32r, WORK + 16 * KB)
        silu = at("silu", [P, F], f32, WORK + 20 * KB)
        hid = at("hid", [P, KF, P], f32, WORK + 22 * KB)
        h_hi = at("h_hi", [P, KF, P], f32r, WORK + 24 * KB)
        h_lo = at("h_lo", [P, KF, P], f32r, WORK + 26 * KB)
        ysb = at("ysb", [P, D], f32, WORK + 28 * KB)
        XS = 3
        xs = [at(f"xs{n}", [P, XS, D], bf16, HI + n * XS * 2 * KB) for n in range(3)]
        x_rest = at("x_rest", [P, D], f32, HI + 3 * XS * 2 * KB)
        pw_hi = at("pw_hi", [P, KD, 2 * P], f32r, MIX)
        pw_lo = at("pw_lo", [P, KD, 2 * P], f32r, MIX + 8 * KB)
        pt_hi = [at(f"pt_hi{n}", [P, KD, P], f32r, where) for n, where in enumerate((MIX + 16 * KB, WORK + 28 * KB))]
        pt_lo = [at(f"pt_lo{n}", [P, KD, P], f32r, where) for n, where in enumerate((MIX + 20 * KB, NFIN))]
        nx = at("nx", [P, 2, KD, P], f32, WORK)
        band0 = at("band0", [P, NG, P], bf16, WORK)
        nxT = at("nxT", [P, 2, KD, P], f32, WORK + 8 * KB)
        band = at("band", [P, NG, P], bf16, WORK + 16 * KB)
        halo = at("halo", [P, NG, HALO], bf16, WORK + 18 * KB)
        wr = at("wr", [P, KD, NL], f32, WORK + 18 * KB + 256)
        tri = at("tri", [P, P], bf16, WORK + 19 * KB + 512)
        ones = at("ones", [P, P], bf16, WORK + 19 * KB + 768)
        iota_p = at("iota_p", [P, P], bf16, WORK + 20 * KB)
        iota_b = at("iota_b", [P, BLOCKS], f32, WORK + 20 * KB + 256)
        tile_no = at("tile_no", [P, K * TILES], f32, WORK + 20 * KB + 448)
        part_no = at("part_no", [P, 1], f32, WORK + 20 * KB + 512)
        steps7 = at("steps7", [P, OVERFLOW // 2], f32, WORK + 20 * KB + 544)
        junk = at("junk", [P, D], bf16, WORK + 22 * KB)
        nf_all = at("nf_all", [P, D], f32, WORK + 24 * KB)
        pw_in = at("pw_in", [P, KD, 2 * P], f32, RW)
        pw = at("pw", [P, KD, 2 * P], f32, RW + 8 * KB)
        sc_all = at("sc_all", [P, D], f32, RW + 16 * KB)
        nm_rows = at("nm_rows", [KD, P], f32, RW + 22 * KB + 768)
        wr_g = at("wr_g", [P, KD * NG], f32, WORK + 4 * KB)
        wr_e = at("wr_e", [P, KD * E], f32, WORK + 4 * KB + 128)
        cursor = [0, 0]

        def room(first, last):
            cursor[0], cursor[1] = first, last

        def tmp(name, shape, dt=f32):
            size = int(np.prod(shape)) * (2 if dt == bf16 else 4)
            here = cursor[0]
            cursor[0] += (size + 31) // 32 * 32
            assert cursor[0] <= cursor[1], name
            return at(name, [P] + list(shape), dt, here)

        KT = K * TILES
        room(WORK + 8 * KB, WORK + 16 * KB)
        pick = tmp("pick", [K, TILES, E])
        prod = tmp("prod", [K, TILES, E])
        part_of = tmp("part_of", [KT, BLOCKS], bf16)
        room(WORK + 28 * KB, WORK + 32 * KB)
        is_row = tmp("is_row", [KT, P], bf16)
        room(WORK + 24 * KB, WORK + 28 * KB)
        byg = tmp("byg", [TILES, NG, NJ])
        over = tmp("over", [E, OVERFLOW // 2])
        is_blk = tmp("is_blk", [KT, BLOCKS], bf16)
        room(WORK + 22 * KB, WORK + 24 * KB)
        t32 = [tmp(f"t32_{n}", [TILES, NG]) for n in range(2)]
        first_g = tmp("first_g", [TILES, NG])
        t64 = [tmp(f"t64_{n}", [TILES, NJ]) for n in range(5)]
        t8 = [tmp(f"t8_{n}", [TILES]) for n in range(8)]
        room(WORK + 20 * KB + 576, WORK + 22 * KB)
        chosen = tmp("chosen", [TILES + 1, E], bf16)
        PAD = E // 2
        run = [tmp(f"run{n}", [PAD + E]) for n in range(2)]
        e32 = [tmp(f"e32_{n}", [E]) for n in range(2)]
        room(WORK + 16 * KB, WORK + 18 * KB)
        tile_of = tmp("tile_of", [KT, BLOCKS], bf16)
        gate_of = [at(f"gate_of{n}", [P, KT, BLOCKS], bf16, where)
                   for n, where in enumerate((NFIN, NFIN + 1536, WORK + 24 * KB + 256))]
        late = at("late", [P, OVERFLOW + 1, E], bf16, NFIN + 3 * KB)
        late_n = at("late_n", [P, OVERFLOW + 1], f32, WORK + 24 * KB + 128)
        gexp = at("gexp", [P, TILES, NG], f32, WORK + 24 * KB)

        k16 = [small(f"k16_{n}", [P, KT], f32) for n in range(4)]
        k16i = [small(f"k16i_{n}", [P, KT], i32) for n in range(2)]
        row16 = small("row16", [P, KT], bf16)
        slot = [small(f"slot{n}", [P, BLOCKS], f32) for n in range(2)]
        ident = small("ident", [P, P], f32)
        logit = small("logit", [P, TILES, NL], f32)
        bias = small("bias", [P, NL], f32)
        ss = small("ss", [P, TILES], f32)
        rs = small("rs", [P, TILES], f32)
        ss2 = small("ss2", [P, TILES], f32)
        rs2 = small("rs2", [P, TILES], f32)
        count0 = small("count0", [P, NG], f32)
        short0 = small("short0", [P, NG], f32)
        fix0 = small("fix0", [P, NG], f32)
        eps = small("eps", [P, 1], f32)
        nm = small("nm", [P, KD], f32)
        gate = small("gate", [P, KT], f32)
        gate_rest = small("gate_rest", [P, 2, KT], f32)
        gate_part = small("gate_part", [P, 3, KT], bf16)
        gate_all = small("gate_all", [P, BLOCKS], f32)
        gate_now = small("gate_now", [P, 1], f32)
        src_all = small("src_all", [P, BLOCKS], i32)
        src_now = small("src_now", [P, XG], i32)
        dst_now = small("dst_now", [P, 1], i32)
        over_e = small("over_e", [P, OVERFLOW + 1], i32)
        n_over = small("n_over", [P, 1], i32)

        psum = ctx.enter_context(nc.psum_tensor("psum", [P, 8, N], f32))
        bank = lambda b, n=1: psum[:, b:b + n, :].rearrange("p b n -> p (b n)")
        PT, PY, NXT, LG, MISC, SLOTS = bank(0, 2), bank(2, 2), bank(4, 2), bank(6), bank(7), bank(6)
        GU, Y, XT, HT = bank(0, 2), bank(2, 2), bank(4, 2), bank(6)

        x_in = [sem(f"x_in{i}") for i in range(TILES)]
        nm_in = sem("nm_in")
        mix_w_in = sem("mix_w_in")
        router_w_in = sem("router_w_in")
        bias_in = sem("bias_in")
        nf_in = sem("nf_in")
        consts = sem("consts")
        dve_step = sem("dve_step")
        act_step = sem("act_step")
        nm_turned = sem("nm_turned")
        pw_made = sem("pw_made")
        pw_hi_done = sem("pw_hi_done")
        pw_split = sem("pw_split")
        squares = sem("squares")
        scales = sem("scales")
        xs_first = sem("xs_first")
        xs_second = sem("xs_second")
        xs_split = sem("xs_split")
        pooled = sem("pooled")
        pt_hi_done = sem("pt_hi_done")
        pt_split = sem("pt_split")
        mixed = sem("mixed")
        res_made = sem("res_made")
        squares2 = sem("squares2")
        nx_made = sem("nx_made")
        nx_turned = sem("nx_turned")
        nxT_copied = sem("nxT_copied")
        nx_stored = [sem(f"nx_stored{i}") for i in range(2)]
        wr_made = sem("wr_made")
        logits_done = sem("logits_done")
        g_shift = sem("g_shift")
        g_exp = sem("g_exp")
        e_shift = sem("e_shift")
        e_exp = sem("e_exp")
        chosen_made = sem("chosen_made")
        ranked = sem("ranked")
        rows_made = sem("rows_made")
        is_blk_made = sem("is_blk_made")
        tile_of_made = sem("tile_of_made")
        slotted = sem("slotted")
        tables_made = sem("tables_made")
        gate_parts = sem("gate_parts")
        gate_of_made = sem("gate_of_made")
        gates_slotted = sem("gates_slotted")
        gates_made = sem("gates_made")
        res_stored = sem("res_stored")
        over_made = sem("over_made")
        raw_in = [sem(f"raw_in{i}") for i in range(RAW)]
        hi_done = sem("hi_done")
        lo_done = sem("lo_done")
        half_hi_done = sem("half_hi_done")
        half_lo_done = sem("half_lo_done")
        pair_used = sem("pair_used")
        idx_now = sem("idx_now")
        gathered = [sem(f"gathered{i}") for i in range(XG)]
        gate_put = sem("gate_put")
        xg_clear = sem("xg_clear")
        x_turned = sem("x_turned")
        x_hi_done = sem("x_hi_done")
        x_split = sem("x_split")
        silu_done = sem("silu_done")
        hid_made = sem("hid_made")
        hid_turned = sem("hid_turned")
        h_hi_done = sem("h_hi_done")
        h_split = sem("h_split")
        y_copied = sem("y_copied")
        y_stored = sem("y_stored")
        y_in = [sem(f"y_in{i}") for i in range(TILES)]
        nfin_in = sem("nfin_in")
        squares3 = sem("squares3")
        out_made = sem("out_made")
        out_stored = sem("out_stored")

        block = ctx.enter_context(nc.Block())

        MAIN = E * PER_STEP

        def pair(s, j):
            if isinstance(s, int) and s == 0:
                return j
            if isinstance(s, int) and s == E:
                return PER_STEP * E - (PER_STEP - GU_PAIRS) + (j - GU_PAIRS)
            return s * PER_STEP + (j - (PER_STEP - GU_PAIRS))

        def slot_of(s0, j, ring):
            return pair(s0, j) % ring

        def pw_low(eng, h):
            half = slice(h * KD // 2, (h + 1) * KD // 2)
            eng.tensor_tensor(pw_lo[:, half, :], pw[:, half, :], pw_hi[:, half, :].bitcast(f32),
                              ALU.subtract).then_inc(pw_split, 1)

        def landed(q, turn):
            return turn * (16 * UNROLL * PER_STEP // RAW) + 16 * (q // RAW + 1)

        def parts(s0):
            return [j for j in range(PER_STEP) if (j < GU_PAIRS or s0 > 0) and (j >= GU_PAIRS or s0 < E)]

        def main_steps(eng, step, last=2):
            for s in range(PEEL):
                step(s, s, 0)
            with eng.Fori(0, (E + 1 - PEEL - last) // UNROLL) as i:
                for u in range(PEEL, PEEL + UNROLL):
                    step(i * UNROLL + u, u, i)
            for s in range(E + 1 - last, E + 1):
                step(s, s, 0)

        def overflow_blocks(eng, body):
            n = eng.value_load(n_over[0:1, 0:1], min_val=0, max_val=OVERFLOW)
            with eng.If(n):
                with eng.Fori(0, n) as v:
                    body(v)
            return n

        @block.sync
        def _(sp):
            def load_x(i):
                sp.dma_start(res[:, i, :], x_rows[i * P:(i + 1) * P, :]).then_inc(x_in[i], 16)

            load_x(0)
            sp.dma_start(nm_rows[:], norm_mix.rearrange("a (j p) -> (a j) p", p=P)).then_inc(nm_in, 16)
            load_x(1)
            sp.dma_start(pw_in[:], pool_w[0].rearrange("g (j p) d -> p (g j) d", p=P)).then_inc(mix_w_in, 16)
            sp.dma_start(sc_all[:], pool_scale.to_broadcast([P, D])).then_inc(mix_w_in, 16)
            load_x(2)
            sp.dma_start(nf_all[:], norm_ffn.to_broadcast([P, D])).then_inc(nf_in, 16)
            sp.dma_start(wr_g[:], w_rg[0].rearrange("(p k) e -> p (k e)", k=KD)).then_inc(router_w_in, 16)
            sp.dma_start(wr_e[:], w_re[0].rearrange("(p k) e -> p (k e)", k=KD)).then_inc(router_w_in, 16)
            for i in range(3, TILES):
                load_x(i)
            sp.dma_start(bias[:, 0:NG], b_rg.to_broadcast([P, NG])).then_inc(bias_in, 16)
            sp.dma_start(bias[:, NG:NL], b_re.to_broadcast([P, E])).then_inc(bias_in, 16)

            def load(s, s0, j, e):
                q = slot_of(s0, j, RAW)
                src = gu_rows if j < GU_PAIRS else dn_rows
                c = j if j < GU_PAIRS else j - GU_PAIRS
                sp.dma_start(raw[q][:], src[bass.ds(e, 1), :, c * PAIR:(c + 1) * PAIR]
                             .rearrange("a p n -> (a p) n")).then_inc(raw_in[q], 16)

            def step(s, s0, turn):
                for j in parts(s0):
                    if isinstance(s, int) and pair(s, j) == RW_SLOT:
                        sp.wait_ge(pw_split, 2)
                    if isinstance(s, int) and RES_SLOT <= pair(s, j) < MIX_SLOT:
                        for i in (2 * (pair(s, j) - RES_SLOT), 2 * (pair(s, j) - RES_SLOT) + 1):
                            sp.wait_ge(res_made, i + 1)
                            sp.dma_start(total[i * P:(i + 1) * P, :], res[:, i, :])\
                                .then_inc(res_stored, 16)
                        sp.wait_ge(nx_made, i + 1)
                        sp.wait_ge(res_stored, 16 * (i + 1))
                    if isinstance(s, int) and pair(s, j) == MIX_SLOT:
                        sp.wait_ge(mixed, TILES)
                    if not (isinstance(s, int) and pair(s, j) < RAW):
                        sp.wait_ge(pair_used, pair(s, j) - RAW + 1)
                    before = pair(s0, j) - FLIGHT
                    if before >= 0:
                        sp.wait_ge(raw_in[before % RAW], landed(before, turn))
                    load(s, s0, j, s if j < GU_PAIRS else s - 1)

            main_steps(sp, step)
            sp.wait_ge(gates_slotted, 1)
            sp.dma_start(nfin[:], norm_final.rearrange("(a d) -> a d", a=1).to_broadcast([P, D]))\
                .then_inc(nfin_in, 16)

            sp.wait_ge(over_made, 1)
            n = sp.value_load(n_over[0:1, 0:1], min_val=0, max_val=OVERFLOW)
            with sp.If(n):
                with sp.Fori(0, n) as v:
                    e = sp.value_load(over_e[0:1, bass.ds(v, 1)], min_val=0, max_val=E - 1)
                    for j in range(PER_STEP):
                        sp.wait_ge(pair_used, v * PER_STEP + (MAIN - PER_STEP + j + 1))
                        src = gu_rows if j < GU_PAIRS else dn_rows
                        c = j if j < GU_PAIRS else j - GU_PAIRS
                        sp.dma_start(raw[j][:], src[bass.ds(e, 1), :, c * PAIR:(c + 1) * PAIR]
                                     .rearrange("a p n -> (a p) n")).then_inc(raw_in[j], 16)
            sp.wait_ge(y_stored, n * 16 + 16 * E)
            for i in range(TILES):
                sp.dma_start(raw[i][:, 0:D], total[i * P:(i + 1) * P, :]).then_inc(y_in[i], 16)
            for i in range(TILES):
                sp.wait_ge(out_made, i + 1)
                sp.dma_start(out_rows[i * P:(i + 1) * P, :], raw[i][:, D:2 * D]).then_inc(out_stored, 16)
            sp.wait_ge(out_stored, 16 * TILES)

        @block.gpsimd
        def _(pool):
            chain = [0]

            def link(ins):
                chain[0] += 1
                ins.then_inc(consts, 1)
                pool.wait_ge(consts, chain[0])

            nc.gpsimd.memset(eps[:], EPS)
            nc.gpsimd.memset(ident[:], 0.0)
            nc.gpsimd.memset(band[:], 1.0)
            nc.gpsimd.memset(halo[:], 1.0)
            nc.gpsimd.iota(count0[:], [[0, NG]], base=1, channel_multiplier=1,
                           allow_small_or_imprecise_dtypes=True)
            link(nc.gpsimd.memset(tri[:], 1.0))
            nc.gpsimd.affine_select(out=ident[:], in_=ident[:], compare_op=ALU.not_equal, fill=1.0,
                                    base=0, pattern=[[-1, P]], channel_multiplier=1)
            link(nc.gpsimd.affine_select(out=band[:], in_=band[:], compare_op=ALU.is_ge, fill=0.0,
                                         base=0, pattern=[[0, NG], [1, P]], channel_multiplier=-1))
            for g, w in enumerate(WINDOWS):
                last = nc.gpsimd.affine_select(out=band[:, g, :], in_=band[:, g, :],
                                               compare_op=ALU.is_ge, fill=0.0, base=w - 1,
                                               pattern=[[-1, P]], channel_multiplier=1)
            link(last)
            for g, w in enumerate(WINDOWS):
                last = nc.gpsimd.affine_select(out=band[:, g, :], in_=band[:, g, :],
                                               compare_op=ALU.not_equal, fill=1.0 - w, base=0,
                                               pattern=[[-1, P]], channel_multiplier=1)
            link(last)
            for g, w in enumerate(WINDOWS):
                nc.gpsimd.affine_select(out=halo[:, g, :], in_=halo[:, g, :], compare_op=ALU.is_ge,
                                        fill=0.0, base=w - 1 - P, pattern=[[-1, HALO]],
                                        channel_multiplier=1)
            nc.gpsimd.affine_select(out=tri[:], in_=tri[:], compare_op=ALU.is_gt, fill=0.0,
                                    base=0, pattern=[[1, P]], channel_multiplier=-1)
            nc.gpsimd.iota(iota_p[:], [[1, P]], base=0, channel_multiplier=0,
                           allow_small_or_imprecise_dtypes=True)
            nc.gpsimd.iota(iota_b[:], [[1, BLOCKS]], base=0, channel_multiplier=0,
                           allow_small_or_imprecise_dtypes=True)
            nc.gpsimd.iota(tile_no[:], [[0, K], [P, TILES]], base=0, channel_multiplier=0,
                           allow_small_or_imprecise_dtypes=True)
            nc.gpsimd.iota(part_no[:], [[0, 1]], base=1, channel_multiplier=1,
                           allow_small_or_imprecise_dtypes=True)
            nc.gpsimd.iota(steps7[:], [[P, OVERFLOW // 2]], base=P, channel_multiplier=0,
                           allow_small_or_imprecise_dtypes=True)
            nc.gpsimd.memset(run[0][:], 0.0)
            nc.gpsimd.memset(run[1][:], 0.0)
            nc.gpsimd.memset(chosen[:], 0.0)
            link(nc.gpsimd.memset(ones[:], 1.0))

            def store(i):
                pool.wait_ge(nx_made, i + 1)
                pool.dma_start(normed[i * P:(i + 1) * P, :], nx[:, i % 2, :, :].rearrange("p k t -> p (k t)"))\
                    .then_inc(nx_stored[i % 2], 16)

            def split_rest(i):
                pool.wait_ge(xs_second, i + 1)
                nc.gpsimd.tensor_tensor(xs[2][:, i % XS, :], x_rest[:], xs[1][:, i % XS, :], ALU.subtract)\
                    .then_inc(xs_split, 1)

            split_rest(0)
            pool.wait_ge(pw_hi_done, 1)
            pw_low(nc.gpsimd, 0)
            split_rest(1)
            for i in range(TILES + 1):
                if i + 2 < TILES:
                    split_rest(i + 2)
                if i >= 1:
                    store(i - 1)

            for par in range(2):
                pool.wait_ge(nx_stored[par], 16 * (TILES // 2))
            pool.wait_ge(nx_turned, TILES)
            nc.gpsimd.memset(xg[:, 0:XG - 1, :], 0.0).then_inc(xg_clear, 1)
            pool.wait_ge(is_blk_made, 1)
            hot = [P, KT, BLOCKS]
            nc.gpsimd.tensor_tensor(tile_of[:], is_blk[:], tile_no[:].unsqueeze(2).to_broadcast(hot),
                                    ALU.mult).then_inc(tile_of_made, 1)
            nc.gpsimd.memset(xg[:, XG - 1, :], 0.0).then_inc(xg_clear, 1)
            pool.wait_ge(xg_clear, 2)
            pool.wait_ge(tables_made, 1)

            def last_row(s, more):
                return TOKENS - 1 if isinstance(s, int) else pool.snap((s | (more * TOKENS - 1)) & (TOKENS - 1))

            def column(s):
                return slice(s, s + 1) if isinstance(s, int) else bass.ds(s, 1)

            def gather(s, g, copies):
                nc.gpsimd.tensor_copy(src_now[:, g:g + 1], src_all[:, column(s)]).then_inc(idx_now, 1)
                pool.wait_ge(idx_now, copies)
                pool.indirect_dma_start(
                    out=xg[:, g, :], out_offset=None, in_=normed[:, :],
                    in_offset=bass.IndirectOffsetOnAxis(ap=src_now[:, g:g + 1].bitcast(u32), axis=0),
                    bounds_check=last_row(s, 1), oob_is_err=False).then_inc(gathered[g], 16)

            def scatter(s, copies):
                if isinstance(s, int) and s == 0:
                    pool.wait_ge(res_stored, 16 * TILES)
                    pool.wait_ge(gates_made, 1)
                else:
                    pool.wait_ge(y_stored, s * 16)
                nc.gpsimd.tensor_copy(gate_now[:], gate_all[:, column(s)]).then_inc(gate_put, 1)
                nc.gpsimd.tensor_copy(dst_now[:], src_all[:, column(s)]).then_inc(idx_now, 1)
                pool.wait_ge(idx_now, copies)
                pool.wait_ge(y_copied, s + 1)
                pool.indirect_dma_start(
                    out=total[:, :],
                    out_offset=bass.IndirectOffsetOnAxis(ap=dst_now[:].bitcast(u32), axis=0),
                    in_=ysb[:], in_offset=None,
                    bounds_check=last_row(s, 2), oob_is_err=False,
                    compute_op=ALU.add).then_inc(y_stored, 16)

            for s in range(XG):
                gather(s, s, s + 1)
            pool.wait_ge(gate_parts, 1)
            for n in range(3):
                last = nc.gpsimd.tensor_tensor(gate_of[n][:], is_blk[:],
                                               gate_part[:, n, :].unsqueeze(2).to_broadcast(hot), ALU.mult)
            last.then_inc(gate_of_made, 1)

            def step(s, s0, turn):
                if s0 < E - XG:
                    pool.wait_ge(x_turned, s + 1)
                    gather(s + XG, s0 % XG, s * 2 + (XG if s0 else XG + 1))
                if s0 > 0:
                    scatter(s - 1, s * 2 + XG + 1 if s0 < E - XG else E + s)

            main_steps(pool, step, 2 + UNROLL)

            pool.wait_ge(over_made, 1)
            n = pool.value_load(n_over[0:1, 0:1], min_val=0, max_val=OVERFLOW)
            with pool.If(n):
                with pool.Fori(0, n) as v:
                    pool.wait_ge(x_turned, v + E)
                    gather(v + E, 0, v * 2 + (2 * E + 1))
                    scatter(v + E, v * 2 + (2 * E + 2))

        @block.scalar
        def _(act):
            chain = [0]

            def root_mean_square(where, rows, i, sums, roots):
                chain[0] += 1
                nc.scalar.activation(where, rows, ACT.Square, accum_out=sums[:, i:i + 1])\
                    .then_inc(act_step, 1)
                act.wait_ge(act_step, chain[0])
                return nc.scalar.activation(roots[:, i:i + 1], sums[:, i:i + 1], ACT.Sqrt,
                                            scale=1.0 / D, bias=eps[:])

            def square(i):
                act.wait_ge(x_in[i], 16)
                root_mean_square(junk[:], res[:, i, :], i, ss, rs).then_inc(squares, 1)

            def split_x(i):
                act.wait_ge(scales, i + 1)
                if i >= XS:
                    act.wait_ge(pooled, i - XS + 2)
                nc.scalar.activation(xs[0][:, i % XS, :], res[:, i, :], ACT.Identity,
                                     scale=rs[:, i:i + 1]).then_inc(xs_first, 1)

            def split_pooled(i):
                act.wait_ge(pooled, i + 1)
                if i >= 2:
                    act.wait_ge(mixed, i - 1)
                nc.scalar.activation(pt_hi[i % 2][:].rearrange("p k t -> p (k t)"), PT, ACT.Copy)\
                    .then_inc(pt_hi_done, 1)

            def square_2(i):
                act.wait_ge(res_made, i + 1)
                root_mean_square(junk[:], res[:, i, :], i, ss2, rs2).then_inc(squares2, 1)

            def copy_turned(i):
                act.wait_ge(nx_turned, i + 1)
                if i >= 2:
                    act.wait_ge(logits_done, i - 1)
                nc.scalar.activation(nxT[:, i % 2, :, :].rearrange("p k t -> p (k t)"), NXT, ACT.Copy)\
                    .then_inc(nxT_copied, 1)

            act.wait_ge(consts, 1)
            square(0)
            split_x(0)
            square(1)
            split_x(1)
            for h in range(2):
                act.wait_ge(pw_made, h + 1)
                half = slice(h * KD // 2, (h + 1) * KD // 2)
                nc.scalar.activation(pw_hi[:, half, :], pw[:, half, :], ACT.Copy).then_inc(pw_hi_done, 1)
            split_pooled(0)
            square(2)
            for i in range(TILES + 2):
                if i + 2 < TILES:
                    split_x(i + 2)
                if 1 <= i <= TILES:
                    square_2(i - 1)
                if i >= 2:
                    copy_turned(i - 2)
                if i + 1 < TILES:
                    split_pooled(i + 1)
                if i + 3 < TILES:
                    square(i + 3)

            def router_exps():
                act.wait_ge(g_shift, 1)
                nc.scalar.activation(gexp[:], t32[0][:], ACT.Exp).then_inc(g_exp, 1)
                act.wait_ge(e_shift, 1)
                nc.scalar.activation(t8[3][:], t8[2][:], ACT.Exp).then_inc(e_exp, 1)

            def split_pair(s, s0, j, use):
                q = slot_of(s0, j, RAW)
                act.wait_ge(raw_in[q], use)
                if not (isinstance(s, int) and pair(s, j) < SPLIT):
                    act.wait_ge(pair_used, pair(s, j) - SPLIT + 1)
                r = slot_of(s0, j, SPLIT)
                if s0 == E and j == PER_STEP - 1:
                    nc.scalar.activation(w_hi[:, r, 0:D], raw[q][:, 0:D], ACT.Copy).then_inc(half_hi_done, 1)
                    nc.scalar.activation(w_hi[:, r, D:PAIR], raw[q][:, D:PAIR], ACT.Copy).then_inc(hi_done, 1)
                else:
                    nc.scalar.activation(w_hi[:, r, :], raw[q][:], ACT.Copy).then_inc(hi_done, 1)

            def split_x_block(s):
                act.wait_ge(x_turned, s + 1)
                nc.scalar.activation(x_hi[:].rearrange("p k t -> p (k t)"), XT, ACT.Copy)\
                    .then_inc(x_hi_done, 1)

            def silu_block(s, gu_end):
                act.wait_ge(pair_used, gu_end)
                if not (isinstance(s, int) and s == 0):
                    act.wait_ge(hid_made, s)
                nc.scalar.activation(silu[:], GU[:, 0:F], ACT.Silu).then_inc(silu_done, 1)

            def split_h_block(s, dn_end):
                act.wait_ge(hid_turned, s + 1)
                if dn_end is not None:
                    act.wait_ge(pair_used, dn_end)
                nc.scalar.activation(h_hi[:].rearrange("p k t -> p (k t)"), HT, ACT.Copy)\
                    .then_inc(h_hi_done, 1)

            def copy_y(s, dn_end):
                act.wait_ge(pair_used, dn_end)
                if not (isinstance(s, int) and s == 0):
                    act.wait_ge(y_stored, s * 16)
                act.wait_ge(gate_put, s + 1)
                nc.scalar.activation(ysb[:], Y, ACT.Identity, scale=gate_now[:]).then_inc(y_copied, 1)

            def step(s, s0, turn):
                js = parts(s0)
                for j in js:
                    if s0 == 0 and j == 0:
                        act.wait_ge(mixed, TILES)
                    if s0 == 0 and j == SPLIT:
                        router_exps()
                    if s0 >= 1 and j == (1 if s0 == 1 else js[0]):
                        silu_block(s - 1, pair(s - 1, GU_PAIRS - 1) + 1 if s0 > 1 else GU_PAIRS)
                        if s0 < E:
                            split_x_block(s)
                    if s0 == 0 and j == 2:
                        split_x_block(s)
                    if s0 >= 1 and j == (2 if s0 < E else PER_STEP - 1):
                        split_h_block(s - 1, None if s0 == 1 else pair(s - 1, PER_STEP - 1) + 1)
                    if s0 == E and j == PER_STEP - 1:
                        copy_y(s - 2, pair(s - 1, PER_STEP - 1) + 1)
                    split_pair(s, s0, j, landed(pair(s0, j), turn))
                    if 2 <= s0 < E and j == 2:
                        copy_y(s - 2, pair(s - 1, PER_STEP - 1) + 1)

            main_steps(act, step)
            copy_y(E - 1, MAIN)

            act.wait_ge(over_made, 1)
            n = act.value_load(n_over[0:1, 0:1], min_val=0, max_val=OVERFLOW)
            with act.If(n):
                with act.Fori(0, n) as v:
                    first = v * PER_STEP + MAIN

                    def over_pair(j):
                        act.wait_ge(raw_in[j], v * 16 + 16 * ((MAIN - 1 - j) // RAW + 2))
                        act.wait_ge(pair_used, first + (j - SPLIT + 1))
                        nc.scalar.activation(w_hi[:, j % SPLIT, :], raw[j][:], ACT.Copy)\
                            .then_inc(hi_done, 1)

                    split_x_block(v + E)
                    for j in range(GU_PAIRS):
                        over_pair(j)
                    silu_block(v + E, first + GU_PAIRS)
                    split_h_block(v + E, first)
                    for j in range(GU_PAIRS, PER_STEP):
                        over_pair(j)
                    copy_y(v + E, first + PER_STEP)

            for i in range(TILES):
                act.wait_ge(y_in[i], 16)
                root_mean_square(junk[:], raw[i][:, 0:D], i, ss, rs).then_inc(squares3, 1)

        @block.vector
        def _(dve):
            chain = [0]

            def link(ins):
                chain[0] += 1
                ins.then_inc(dve_step, 1)
                dve.wait_ge(dve_step, chain[0])

            V = nc.vector

            def scale_x(i):
                dve.wait_ge(squares, i + 1)
                V.reciprocal(rs[:, i:i + 1], rs[:, i:i + 1]).then_inc(scales, 1)

            def make_rest(i):
                dve.wait_ge(xs_first, i + 1)
                if i >= 1:
                    dve.wait_ge(xs_split, i)
                link(V.scalar_tensor_tensor(x_rest[:], res[:, i, :], rs[:, i:i + 1], xs[0][:, i % XS, :],
                                            ALU.mult, ALU.subtract))
                V.tensor_copy(xs[1][:, i % XS, :], x_rest[:]).then_inc(xs_second, 1)

            def pooled_low(i):
                dve.wait_ge(pt_hi_done, i + 1)
                V.tensor_tensor(pt_lo[i % 2][:].rearrange("p k t -> p (k t)"), PT,
                                pt_hi[i % 2][:].rearrange("p k t -> p (k t)").bitcast(f32), ALU.subtract)\
                    .then_inc(pt_split, 1)

            dve.wait_ge(consts, 4)
            for g, w in enumerate(WINDOWS):
                last = V.tensor_scalar(count0[:, g:g + 1], count0[:, g:g + 1], float(w), None, ALU.min)
            link(last)
            for g, w in enumerate(WINDOWS):
                last = V.tensor_scalar(short0[:, g:g + 1], count0[:, g:g + 1], -1.0, float(w), ALU.mult, ALU.add)
            link(last)
            scale_x(0)
            for g, w in enumerate(WINDOWS):
                V.scalar_tensor_tensor(band0[:, g, :], ident[:], short0[:, g:g + 1], band[:, g, :],
                                       ALU.mult, ALU.add)
            make_rest(0)
            dve.wait_ge(nm_turned, 1)
            for g, w in enumerate(WINDOWS):
                last = V.tensor_scalar(nm[:, 2 * g:2 * g + 2], MISC[:, 2 * g:2 * g + 2], 1.0 / w, None,
                                       ALU.mult)
            link(last)
            scale_x(1)
            dve.wait_ge(mix_w_in, 32)
            for c in range(KD):
                g = c // 2
                last = V.scalar_tensor_tensor(pw[:, c, :], pw_in[:, c, :], nm[:, c:c + 1],
                                              sc_all[:, g * 2 * P:(g + 1) * 2 * P], ALU.mult, ALU.mult)
                if c % (KD // 2) == KD // 2 - 1:
                    last.then_inc(pw_made, 1)
            make_rest(1)
            pooled_low(0)
            dve.wait_ge(pw_hi_done, 2)
            pw_low(V, 1)
            scale_x(2)
            link(V.reciprocal(fix0[:], count0[:]))
            for g, w in enumerate(WINDOWS):
                V.tensor_scalar(fix0[:, g:g + 1], fix0[:, g:g + 1], float(w), None, ALU.mult)

            def add_mixed(i):
                dve.wait_ge(mixed, i + 1)
                if i == 0:
                    for g in range(NG):
                        c = slice(g * 2 * P, (g + 1) * 2 * P)
                        last = V.scalar_tensor_tensor(res[:, i, c], PY[:, c], fix0[:, g:g + 1],
                                                      res[:, i, c], ALU.mult, ALU.add)
                else:
                    last = V.tensor_tensor(res[:, i, :], PY, res[:, i, :], ALU.add)
                last.then_inc(res_made, 1)

            def norm_2(m):
                dve.wait_ge(squares2, m + 1)
                link(V.reciprocal(rs2[:, m:m + 1], rs2[:, m:m + 1]))
                if m >= 2:
                    dve.wait_ge(nx_stored[m % 2], 16 * (m // 2))
                    dve.wait_ge(nx_turned, m - 1)
                V.scalar_tensor_tensor(nx[:, m % 2, :, :].rearrange("t k p -> t p k"),
                                       res[:, m, :].rearrange("t (p k) -> t p k", k=KD),
                                       rs2[:, m:m + 1],
                                       nf_all[:].rearrange("t (p k) -> t p k", k=KD),
                                       ALU.mult, ALU.mult).then_inc(nx_made, 1)

            for i in range(TILES + 1):
                if i >= 1:
                    add_mixed(i - 1)
                if i == 1:
                    dve.wait_ge(router_w_in, 32)
                    V.tensor_copy(wr[:, :, 0:NG], wr_g[:].rearrange("p (k e) -> p k e", k=KD))
                    V.tensor_copy(wr[:, :, NG:NL], wr_e[:].rearrange("p (k e) -> p k e", k=KD))\
                        .then_inc(wr_made, 1)
                    dve.wait_ge(nf_in, 16)
                if i + 2 < TILES:
                    make_rest(i + 2)
                if i >= 1:
                    norm_2(i - 1)
                if i + 1 < TILES:
                    pooled_low(i + 1)
                if i + 3 < TILES:
                    scale_x(i + 3)

            def bc(ap, axis, shape):
                return ap.unsqueeze(axis).to_broadcast(shape)

            dve.wait_ge(logits_done, TILES)
            dve.wait_ge(bias_in, 32)
            link(V.tensor_tensor(logit[:], LG[:, 0:TILES * NL].rearrange("p (i e) -> p i e", e=NL),
                                 bc(bias[:], 1, [P, TILES, NL]), ALU.add))
            gl = logit[:, :, 0:NG]
            el = logit[:, :, NG:NL].rearrange("p i (g j) -> p i g j", g=NG)
            S8, S4 = [P, TILES, NJ], [P, TILES, NG]

            def first_max(onehot, src, top, scratch, n, shape):
                link(V.tensor_reduce(top, src, AX, ALU.max))
                link(V.tensor_tensor(scratch, src, bc(top, 2, shape), ALU.is_lt))
                link(V.scalar_tensor_tensor(scratch, scratch, float(n), bc(iota_b[:, 0:n], 1, shape),
                                            ALU.mult, ALU.add))
                link(V.tensor_reduce(t8[7][:], scratch, AX, ALU.min))
                return V.tensor_tensor(onehot, scratch, bc(t8[7][:], 2, shape), ALU.is_equal)

            link(first_max(first_g[:], gl, t8[0][:], t32[1][:], NG, S4))
            S48 = [P, TILES, NG, NJ]
            link(V.tensor_tensor(byg[:], el, bc(first_g[:], 3, S48), ALU.mult))
            link(V.tensor_reduce(t64[0][:], byg[:].rearrange("p i g j -> p i j g"), AX, ALU.add))
            link(first_max(t64[1][:], t64[0][:], t8[1][:], t64[3][:], NJ, S8))
            V.tensor_tensor(pick[:, 0, :, :].rearrange("p i (g j) -> p i g j", g=NG),
                            bc(first_g[:], 3, S48), bc(t64[1][:], 2, S48), ALU.mult)
            link(V.scalar_tensor_tensor(t64[4][:], t64[1][:], -3.0e38, t64[0][:], ALU.mult, ALU.add))
            link(first_max(t64[2][:], t64[4][:], t8[4][:], t64[3][:], NJ, S8))
            link(V.tensor_tensor(pick[:, 1, :, :].rearrange("p i (g j) -> p i g j", g=NG),
                                 bc(first_g[:], 3, S48), bc(t64[2][:], 2, S48), ALU.mult))
            V.tensor_tensor(chosen[:, 0:TILES, :], pick[:, 0, :, :], pick[:, 1, :, :], ALU.add)\
                .then_inc(chosen_made, 1)
            SK = [P, K, TILES, E]
            by_k = lambda ap: ap.rearrange("p (k i) -> p k i", k=K)
            link(V.tensor_tensor(prod[:], pick[:], iota_b[:, 0:E].unsqueeze(1).unsqueeze(1).to_broadcast(SK),
                                 ALU.mult))
            link(V.tensor_reduce(by_k(k16[0][:]), prod[:], AX, ALU.add))
            dve.wait_ge(ranked, 1)
            counts = MISC[:, TILES * E:(TILES + 1) * E]
            V.tensor_tensor(over[:], bc(counts, 2, [P, E, OVERFLOW // 2]),
                            bc(steps7[:], 1, [P, E, OVERFLOW // 2]), ALU.is_gt)
            link(V.tensor_tensor(prod[:], pick[:],
                                 MISC[:, 0:TILES * E].rearrange("p (i e) -> p i e", e=E).unsqueeze(1)
                                 .to_broadcast(SK), ALU.mult))
            V.tensor_reduce(by_k(k16[1][:]), prod[:], AX, ALU.add)
            link(V.tensor_reduce(run[0][:, PAD:], over[:], AX, ALU.add))
            V.tensor_copy(e32[0][:], run[0][:, PAD:])
            V.tensor_copy(k16i[0][:], k16[1][:])
            a, b, shift = run[0], run[1], 1
            while shift < E:
                link(V.tensor_tensor(b[:, PAD:], a[:, PAD:], a[:, PAD - shift:PAD + E - shift], ALU.add))
                a, b, shift = b, a, shift * 2
            ends = a[:, PAD:]
            V.tensor_scalar(k16i[1][:], k16i[0][:], P - 1, None, ALU.bitwise_and)
            link(V.tensor_tensor(e32[1][:], ends, e32[0][:], ALU.subtract))
            V.tensor_scalar(k16i[0][:], k16i[0][:], 7, None, ALU.logical_shift_right)
            link(V.scalar_tensor_tensor(e32[1][:], e32[1][:], float(E - 1), iota_b[:, 0:E],
                                        ALU.add, ALU.subtract))
            V.tensor_copy(row16[:], k16i[1][:])
            V.tensor_copy(k16[1][:], k16i[0][:])
            link(V.tensor_tensor(prod[:], pick[:], e32[1][:].unsqueeze(1).unsqueeze(1).to_broadcast(SK),
                                 ALU.mult))
            link(V.tensor_reduce(by_k(k16[2][:]), prod[:], AX, ALU.add))
            link(V.scalar_tensor_tensor(k16[3][:], k16[1][:], 0.0, k16[2][:], ALU.is_gt, ALU.mult))
            link(V.tensor_tensor(k16[3][:], k16[3][:], k16[1][:], ALU.add))
            link(V.tensor_tensor(k16[3][:], k16[3][:], k16[0][:], ALU.add))
            V.tensor_tensor(is_blk[:], bc(iota_b[:], 1, [P, KT, BLOCKS]), bc(k16[3][:], 2, [P, KT, BLOCKS]),
                            ALU.is_equal).then_inc(is_blk_made, 1)
            V.tensor_tensor(is_row[:], bc(iota_p[:], 1, [P, KT, P]), bc(row16[:], 2, [P, KT, P]),
                            ALU.is_equal)
            dve.wait_ge(is_blk_made, 1)
            V.tensor_scalar(part_of[:], is_blk[:], part_no[:], None, ALU.mult).then_inc(rows_made, 1)
            V.tensor_copy(n_over[:], ends[:, E - 1:E])
            dve.wait_ge(slotted, 1)
            link(V.tensor_copy(slot[0][:], SLOTS[:, 0:BLOCKS]))
            link(V.tensor_scalar(slot[1][:], slot[0][:], 0.0, FAR, ALU.is_equal, ALU.mult))
            V.scalar_tensor_tensor(src_all[:], slot[1][:], -1.0, slot[0][:], ALU.add, ALU.add)\
                .then_inc(tables_made, 1)
            V.tensor_tensor(t32[0][:], gl, bc(t8[0][:], 2, S4), ALU.subtract).then_inc(g_shift, 1)
            V.tensor_tensor(t8[2][:], t8[4][:], t8[1][:], ALU.subtract).then_inc(e_shift, 1)

            def gates():
                link(V.tensor_tensor(late[:], bc(ends, 1, [P, OVERFLOW + 1, E]),
                                     bc(iota_b[:, 0:OVERFLOW + 1], 2, [P, OVERFLOW + 1, E]), ALU.is_le))
                link(V.tensor_reduce(late_n[:], late[:], AX, ALU.add))
                V.tensor_scalar(over_e[:], late_n[:], float(E - 1), None, ALU.min).then_inc(over_made, 1)
                dve.wait_ge(g_exp, 1)
                link(V.tensor_reduce(t8[5][:], gexp[:], AX, ALU.add))
                dve.wait_ge(e_exp, 1)
                link(V.scalar_tensor_tensor(t8[6][:], t8[3][:], 1.0, t8[5][:], ALU.add, ALU.mult))
                link(V.reciprocal(gate[:, 0:TILES], t8[6][:]))
                link(V.tensor_tensor(gate[:, TILES:KT], gate[:, 0:TILES], t8[3][:], ALU.mult))
                left = gate[:]
                for n in range(3):
                    last = V.tensor_copy(gate_part[:, n, :], left)
                    if n < 2:
                        link(last)
                        link(V.tensor_tensor(gate_rest[:, n, :], left, gate_part[:, n, :], ALU.subtract))
                        left = gate_rest[:, n, :]
                last.then_inc(gate_parts, 1)

            def low_pair(s, s0, j):
                q, r = slot_of(s0, j, RAW), slot_of(s0, j, SPLIT)

                def low(c0, c1):
                    return V.tensor_tensor(w_lo[q][:, c0:c1], raw[q][:, c0:c1],
                                           w_hi[:, r, c0:c1].bitcast(f32), ALU.subtract)

                if s0 == E and j == PER_STEP - 1:
                    dve.wait_ge(half_hi_done, 1)
                    low(0, D).then_inc(half_lo_done, 1)
                    dve.wait_ge(hi_done, pair(s, j) + 1)
                    low(D, PAIR).then_inc(lo_done, 1)
                else:
                    dve.wait_ge(hi_done, pair(s, j) + 1)
                    low(0, PAIR).then_inc(lo_done, 1)

            def low_x(s):
                dve.wait_ge(x_hi_done, s + 1)
                V.tensor_tensor(x_lo[:].rearrange("p k t -> p (k t)"), XT,
                                x_hi[:].rearrange("p k t -> p (k t)").bitcast(f32), ALU.subtract)\
                    .then_inc(x_split, 1)

            def hidden(s):
                dve.wait_ge(silu_done, s + 1)
                if not (isinstance(s, int) and s == 0):
                    dve.wait_ge(hid_turned, s)
                V.tensor_tensor(hid[:].rearrange("t k p -> t p k"),
                                silu[:].rearrange("t (p k) -> t p k", k=KF),
                                GU[:, F:2 * F].rearrange("t (p k) -> t p k", k=KF), ALU.mult)\
                    .then_inc(hid_made, 1)

            def low_h(s):
                dve.wait_ge(h_hi_done, s + 1)
                V.tensor_tensor(h_lo[:].rearrange("p k t -> p (k t)"), HT,
                                h_hi[:].rearrange("p k t -> p (k t)").bitcast(f32), ALU.subtract)\
                    .then_inc(h_split, 1)

            def step(s, s0, turn):
                js = parts(s0)
                for j in js:
                    if s0 >= 1 and j == (1 if s0 == 1 else js[0]):
                        hidden(s - 1)
                        if s0 < E:
                            low_x(s)
                    if s0 == 0 and j == 2:
                        low_x(s)
                    if s0 == 0 and j == SPLIT:
                        gates()
                    if s0 == 1 and j == 0:
                        dve.wait_ge(gates_slotted, 1)
                        V.tensor_copy(gate_all[:], MISC[:, 0:BLOCKS]).then_inc(gates_made, 1)
                    if s0 >= 1 and j == (2 if s0 < E else PER_STEP - 1):
                        low_h(s - 1)
                    low_pair(s, s0, j)

            main_steps(dve, step)

            dve.wait_ge(over_made, 1)
            n = dve.value_load(n_over[0:1, 0:1], min_val=0, max_val=OVERFLOW)
            with dve.If(n):
                with dve.Fori(0, n) as v:
                    def over_pair(j):
                        dve.wait_ge(hi_done, v * PER_STEP + (MAIN + j + 1))
                        V.tensor_tensor(w_lo[j][:], raw[j][:],
                                        w_hi[:, j % SPLIT, :].bitcast(f32), ALU.subtract)\
                            .then_inc(lo_done, 1)

                    low_x(v + E)
                    for j in range(GU_PAIRS):
                        over_pair(j)
                    hidden(v + E)
                    low_h(v + E)
                    for j in range(GU_PAIRS, PER_STEP):
                        over_pair(j)

            dve.wait_ge(nfin_in, 16)
            for i in range(TILES):
                dve.wait_ge(squares3, i + 1)
                link(V.reciprocal(rs[:, i:i + 1], rs[:, i:i + 1]))
                V.scalar_tensor_tensor(raw[i][:, D:2 * D], raw[i][:, 0:D], rs[:, i:i + 1], nfin[:],
                                       ALU.mult, ALU.mult).then_inc(out_made, 1)

        @block.tensor
        def _(pe):
            mm = nc.tensor.matmul

            pe.wait_ge(consts, 2)
            pe.wait_ge(nm_in, 16)
            nc.tensor.transpose(MISC[:, 0:KD], nm_rows[:], ident[0:KD, 0:KD]).then_inc(nm_turned, 1)

            def pool_tile(i):
                pe.wait_ge(xs_split, i + 1)
                if i >= 1:
                    pe.wait_ge(pt_split, i)
                for c in range(KD):
                    cols = slice(c * P, (c + 1) * P)
                    terms = [(x, i % XS, (band if i else band0)[:, c // 2, :], c * P, P) for x in xs]
                    if i:
                        terms += [(x, (i - 1) % XS, halo[:, c // 2, :], c * P, HALO) for x in xs]
                    for n, (x, par, mask, c0, width) in enumerate(terms):
                        last = mm(PT[:, c0:c0 + width], x[:, par, cols], mask,
                                  start=(n == 0), stop=(n == len(terms) - 1))
                last.then_inc(pooled, 1)

            def mix_tile(i):
                pe.wait_ge(pt_split, i + 1)
                if i == 0:
                    pe.wait_ge(pw_split, 2)
                if i >= 1:
                    pe.wait_ge(res_made, i)
                for g in range(NG):
                    terms = [(a, b, c) for c in (2 * g, 2 * g + 1)
                             for a, b in ((pt_hi[i % 2], pw_hi), (pt_hi[i % 2], pw_lo), (pt_lo[i % 2], pw_hi))]
                    for n, (a, b, c) in enumerate(terms):
                        last = mm(PY[:, g * 2 * P:(g + 1) * 2 * P], a[:, c, :], b[:, c, :],
                                  start=(n == 0), stop=(n == len(terms) - 1))
                last.then_inc(mixed, 1)

            def turn_tile(i):
                pe.wait_ge(nx_made, i + 1)
                if i >= 1:
                    pe.wait_ge(nxT_copied, i)
                for c in range(KD):
                    last = nc.tensor.transpose(NXT[:, c * P:(c + 1) * P], nx[:, i % 2, c, :], ident[:])
                last.then_inc(nx_turned, 1)

            def logits_tile(i):
                pe.wait_ge(nxT_copied, i + 1)
                if i == 0:
                    pe.wait_ge(wr_made, 1)
                for c in range(KD):
                    last = mm(LG[:, i * NL:(i + 1) * NL], nxT[:, i % 2, c, :], wr[:, c, :],
                              start=(c == 0), stop=(c == KD - 1))
                last.then_inc(logits_done, 1)

            def keep_warm(n, where=PY):
                for _ in range(n):
                    mm(where[:, 0:P], ident[:], ident[:], start=True, stop=True)

            pool_tile(0)
            for i in range(TILES + 2):
                if i + 1 < TILES:
                    pool_tile(i + 1)
                if i < TILES:
                    mix_tile(i)
                if i == TILES + 1:
                    keep_warm(5, MISC)
                if i >= 2:
                    logits_tile(i - 2)
                if i == TILES:
                    keep_warm(5, MISC)
                if 1 <= i <= TILES:
                    turn_tile(i - 1)

            keep_warm(28)
            pe.wait_ge(chosen_made, 1)
            pe.wait_ge(consts, 5)
            flat = chosen[:].rearrange("p i e -> p (i e)")
            mm(MISC[:, 0:(TILES + 1) * E], tri[:], flat, start=True, stop=False)
            for i in range(TILES):
                last = mm(MISC[:, (i + 1) * E:(TILES + 1) * E].rearrange("p (i e) -> p i e", e=E), ones[:],
                          chosen[:, i:i + 1, :].to_broadcast([P, TILES - i, E]),
                          start=False, stop=(i == TILES - 1))
            last.then_inc(ranked, 1)
            keep_warm(36)
            pe.wait_ge(rows_made, 1)
            pe.wait_ge(tile_of_made, 1)
            for n in range(KT):
                for hot in (part_of, tile_of):
                    last = mm(SLOTS[:, 0:BLOCKS], is_row[:, n, :], hot[:, n, :],
                              start=(n == 0 and hot is part_of), stop=(n == KT - 1 and hot is tile_of))
            last.then_inc(slotted, 1)

            def products(dst, hi, lo, j0, chunks, slot, raw_slot, cs=(0, 1)):
                for c in cs:
                    ch = j0 + c
                    b_hi, b_lo = w_hi[:, slot, :], w_lo[raw_slot][:]
                    for a, b in ((hi, b_hi), (hi, b_lo), (lo, b_hi)):
                        for n in range(2):
                            last = mm(dst[:, n * N:(n + 1) * N], a[:, ch, :],
                                      b[:, c * D + n * N:c * D + (n + 1) * N],
                                      start=(ch == 0 and a is hi and b is b_hi),
                                      stop=(ch == chunks - 1 and a is lo))
                return last

            def slot_gates():
                pe.wait_ge(gate_of_made, 1)
                for n in range(KT):
                    for m in range(3):
                        last = mm(MISC[:, 0:BLOCKS], is_row[:, n, :], gate_of[m][:, n, :],
                                  start=(n == 0 and m == 0), stop=(n == KT - 1 and m == 2))
                last.then_inc(gates_slotted, 1)

            def turn_x(s, g, landed):
                pe.wait_ge(gathered[g], landed)
                if not (isinstance(s, int) and s == 0):
                    pe.wait_ge(x_split, s)
                for c in range(KD):
                    last = nc.tensor.transpose(XT[:, c * P:(c + 1) * P],
                                               xg[:, g, c * P:(c + 1) * P], ident[:])
                last.then_inc(x_turned, 1)

            def turn_h(s):
                pe.wait_ge(hid_made, s + 1)
                if not (isinstance(s, int) and s == 0):
                    pe.wait_ge(h_split, s)
                for c in range(KF):
                    last = nc.tensor.transpose(HT[:, c * P:(c + 1) * P], hid[:, c, :], ident[:])
                last.then_inc(hid_turned, 1)

            def gu_pair(s, j, q, slot, raw_slot):
                if j == 0:
                    pe.wait_ge(x_split, s + 1)
                    if not (isinstance(s, int) and s == 0):
                        pe.wait_ge(hid_made, s)
                pe.wait_ge(lo_done, q + 1)
                products(GU, x_hi, x_lo, 2 * j, KD, slot, raw_slot).then_inc(pair_used, 1)

            def dn_pair(s, j, q, slot, raw_slot):
                if j == 0:
                    pe.wait_ge(h_split, s + 1)
                    if not (isinstance(s, int) and s == 0):
                        pe.wait_ge(y_copied, s)
                cs = (0, 1)
                if isinstance(q, int) and q == MAIN - 1:
                    pe.wait_ge(half_lo_done, 1)
                    products(Y, h_hi, h_lo, 2 * j, KF, slot, raw_slot, (0,))
                    cs = (1,)
                pe.wait_ge(lo_done, q + 1)
                products(Y, h_hi, h_lo, 2 * j, KF, slot, raw_slot, cs).then_inc(pair_used, 1)

            keep_warm(20)
            turn_x(0, 0, 16)
            keep_warm(8)

            def step(s, s0, turn):
                for j in parts(s0):
                    q, r = slot_of(s0, j, SPLIT), slot_of(s0, j, RAW)
                    if j < GU_PAIRS:
                        gu_pair(s, j, pair(s, j), q, r)
                    if s0 == 0 and j == SPLIT:
                        slot_gates()
                    if j == GU_PAIRS - 2 and s0 < E - 1:
                        turn_x(s + 1, (s0 + 1) % XG, turn * 16 + 16 * ((s0 + 1) // XG + 1))
                    if j >= GU_PAIRS:
                        dn_pair(s - 1, j - GU_PAIRS, pair(s, j), q, r)
                    if s0 < E and j == (GU_PAIRS if s0 else GU_PAIRS - 1):
                        turn_h(s)

            main_steps(pe, step)

            pe.wait_ge(over_made, 1)
            n = pe.value_load(n_over[0:1, 0:1], min_val=0, max_val=OVERFLOW)
            with pe.If(n):
                with pe.Fori(0, n) as v:
                    turn_x(v + E, 0, v * 16 + 16 * ((E - 1) // XG + 2))
                    for j in range(GU_PAIRS):
                        gu_pair(v + E, j, v * PER_STEP + (MAIN + j), j % SPLIT, j)
                    turn_h(v + E)
                    for j in range(GU_PAIRS, PER_STEP):
                        dn_pair(v + E, j - GU_PAIRS, v * PER_STEP + (MAIN + j), j % SPLIT, j)


_INS = ["x", "norm_mix", "norm_ffn", "norm_final", "pool_w", "pool_scale", "router_group_w",
        "router_group_b", "router_expert_w", "router_expert_b", "expert_w_gu", "expert_w_down"]


def kernel(**inputs):
    import concourse.bacc as _bacc
    from concourse.bass_utils import run_bass_kernel_spmd as _run

    nc = _bacc.Bacc("TRN2", target_bir_lowering=False, num_devices=1)
    arrays, args = {}, []
    for name in _INS:
        a = np.ascontiguousarray(inputs[name])
        arrays[f"in_{name}"] = a
        args.append(nc.dram_tensor(f"in_{name}", a.shape, mybir.dt.from_np(a.dtype), kind="ExternalInput").ap())
    out = nc.dram_tensor("out", inputs["x"].shape, mybir.dt.float32, kind="ExternalOutput").ap()
    hybrid_pool_moe(nc, *args, out)
    r = _run(nc, [arrays], core_ids=[0])
    return r.results[0]["out"]
```
